# Optimizing a Trainium2 kernel written in Bass

```python
import jax, jax.numpy as jnp
from jax import lax
import numpy as np

D_MODEL = 2048
BATCH = 1
SEQ = 256
DEPTH = 1
DEC_BATCH = 8
DEC_SEQ = 4
PAST_LEN = 2048
PAGE_SIZE = 128

HEAD_DIM = 128
MLSTM_HEADS = 8
GDN_HEADS = 8
MLSTM_WIDTH = MLSTM_HEADS * HEAD_DIM
GDN_WIDTH = GDN_HEADS * HEAD_DIM
MIX_WIDTH = MLSTM_WIDTH + GDN_WIDTH
CONV_W = 4
N_META = 16
CHUNK = 64
D_FF = -(-8 * D_MODEL // (3 * 256)) * 256
EPS = 1e-6
IN_SIZES = (MLSTM_WIDTH,) * 4 + (MLSTM_HEADS,) * 2 + (GDN_WIDTH,) * 4 + (GDN_HEADS,) * 2
IN_COLS = sum(IN_SIZES)

kernel_name = "hymba_mlstm_gdn_decode_step"

def _split_cols(x, sizes):
    out, start = [], 0
    for s in sizes:
        out.append(x[..., start:start + s])
        start += s
    return out

def rmsnorm(x, w):
    xf = x.astype(jnp.float32)
    y = xf * lax.rsqrt(jnp.mean(xf * xf, axis=-1, keepdims=True) + EPS)
    return (y * w.astype(jnp.float32)).astype(x.dtype)

def l2norm(x):
    return x * lax.rsqrt(jnp.sum(x * x, axis=-1, keepdims=True) + EPS)

def causal_conv(x_pre, buf, w):
    T = x_pre.shape[1]
    xp = jnp.concatenate([buf, x_pre], axis=1)
    out = xp[:, 0:T] * w[0]
    for i in range(1, CONV_W):
        out = out + xp[:, i:i + T] * w[i]
    return jax.nn.silu(out), xp[:, -(CONV_W - 1):]

def mlstm_chunk(state, inp):
    C, n, m = state
    q, k, v, li, lf = inp
    L = q.shape[1]
    b = jnp.cumsum(lf, axis=1)
    a = b + m[:, None, :]
    mask = jnp.tril(jnp.ones((L, L), dtype=bool))[None, :, :, None]
    Dm = jnp.where(mask, b[:, :, None, :] - b[:, None, :, :] + li[:, None, :, :], -jnp.inf)
    m_t = jnp.maximum(a, jnp.max(Dm, axis=2))
    inter = jnp.exp(a - m_t)
    W = jnp.exp(Dm - m_t[:, :, None, :])
    s = jnp.einsum('bthd,bjhd->btjh', q, k) * W
    num = jnp.einsum('btjh,bjhe->bthe', s, v) + inter[..., None] * jnp.einsum('bthd,bhde->bthe', q, C)
    den = jnp.sum(s, axis=2) + inter * jnp.einsum('bthd,bhd->bth', q, n)
    h = num / jnp.maximum(jnp.abs(den), jnp.exp(-m_t))[..., None]
    mL = m_t[:, -1]
    wL = jnp.exp(b[:, -1:] - b + li - mL[:, None])
    dC = jnp.exp(b[:, -1] + m - mL)
    C_new = dC[..., None, None] * C + jnp.einsum('bjh,bjhd,bjhe->bhde', wL, k, v)
    n_new = dC[..., None] * n + jnp.einsum('bjh,bjhd->bhd', wL, k)
    return (C_new, n_new, mL), h

def gdn_chunk(S, inp):
    q, k, v, lg, beta = inp
    L = q.shape[1]
    G = jnp.cumsum(lg, axis=1)
    causal = jnp.tril(jnp.ones((L, L), dtype=bool))[None, :, :, None]
    strict = jnp.tril(jnp.ones((L, L), dtype=bool), k=-1)[None, :, :, None]
    diff = G[:, :, None, :] - G[:, None, :, :]
    decay = jnp.where(causal, jnp.exp(jnp.where(causal, diff, 0.0)), 0.0)
    kk = jnp.einsum('bthd,bjhd->btjh', k, k)
    A = jnp.where(strict, beta[:, :, None, :] * kk * decay, 0.0)
    eG = jnp.exp(G)
    rhs = beta[..., None] * (v - eG[..., None] * jnp.einsum('bthd,bhde->bthe', k, S))
    Amat = jnp.transpose(A, (0, 3, 1, 2)) + jnp.eye(L, dtype=A.dtype)
    Wv = lax.linalg.triangular_solve(Amat, jnp.transpose(rhs, (0, 2, 1, 3)),
                                     left_side=True, lower=True, unit_diagonal=True)
    Wv = jnp.transpose(Wv, (0, 2, 1, 3))
    qk = jnp.einsum('bthd,bjhd->btjh', q, k) * decay
    o = eG[..., None] * jnp.einsum('bthd,bhde->bthe', q, S) + jnp.einsum('btjh,bjhe->bthe', qk, Wv)
    GL = G[:, -1]
    S_new = jnp.exp(GL)[..., None, None] * S + jnp.einsum('bjh,bjhd,bjhe->bhde', jnp.exp(GL[:, None] - G), k, Wv)
    return S_new, o

def chunked_scan(fn, state, xs, lead, chunk):
    outs = []
    if lead > 0:
        state, o = fn(state, tuple(t[:, :lead] for t in xs))
        outs.append(o)
        xs = tuple(t[:, lead:] for t in xs)
    B, T = xs[0].shape[:2]
    nc = T // chunk
    blocks = tuple(jnp.moveaxis(t.reshape((B, nc, chunk) + t.shape[2:]), 1, 0) for t in xs)
    state, o = lax.scan(fn, state, blocks)
    o = jnp.moveaxis(o, 0, 1).reshape((B, T) + o.shape[3:])
    outs.append(o)
    return state, jnp.concatenate(outs, axis=1)

def mixer(u, st, w_in, b_i, b_f, m_norm, conv_w, A_log, dt_bias, g_norm, w_out, lead, chunk):
    B, T, _ = u.shape
    f32 = jnp.float32
    C0, n0, m0, S0, buf0 = st
    proj = jnp.einsum('btd,dc->btc', u, w_in).astype(f32)
    mq, mk, mv, mo, mi, mf, gq, gk, gv, gz, ga, gb = _split_cols(proj, IN_SIZES)

    def heads(t):
        return t.reshape(B, T, t.shape[-1] // HEAD_DIM, HEAD_DIM)

    qm = heads(mq) * (HEAD_DIM ** -0.5)
    li = mi + b_i.astype(f32)
    lf = jax.nn.log_sigmoid(mf + b_f.astype(f32))
    (C1, n1, m1), hm = chunked_scan(mlstm_chunk, (C0, n0, m0), (qm, heads(mk), heads(mv), li, lf), lead, chunk)
    hm = rmsnorm(hm, m_norm) * jax.nn.sigmoid(heads(mo))

    qkv, buf1 = causal_conv(jnp.concatenate([gq, gk, gv], axis=-1), buf0, conv_w.astype(f32))
    cq, ck, cv = _split_cols(qkv, (GDN_WIDTH,) * 3)
    qg = l2norm(heads(cq)) * (HEAD_DIM ** -0.5)
    kg = l2norm(heads(ck))
    lg = -jnp.exp(A_log.astype(f32)) * jax.nn.softplus(ga + dt_bias.astype(f32))
    beta = jax.nn.sigmoid(gb)
    S1, og = chunked_scan(gdn_chunk, S0, (qg, kg, heads(cv), lg, beta), lead, chunk)
    og = rmsnorm(og, g_norm) * jax.nn.silu(heads(gz))

    mix = jnp.concatenate([hm.reshape(B, T, MLSTM_WIDTH), og.reshape(B, T, GDN_WIDTH)], axis=-1).astype(u.dtype)
    out = jnp.einsum('btc,cd->btd', mix, w_out)
    return out, (C1, n1, m1, S1, buf1)

def decoder_layer(x, st, norm_pre_mix, norm_post_mix, norm_pre_ffn, norm_post_ffn, w_in, b_i, b_f,
                  m_norm, conv_w, A_log, dt_bias, g_norm, w_out, w_gate_up, w_down, lead, chunk):
    u = rmsnorm(x, norm_pre_mix)
    mo, new_st = mixer(u, st, w_in, b_i, b_f, m_norm, conv_w, A_log, dt_bias, g_norm, w_out, lead, chunk)
    x = x + rmsnorm(mo, norm_post_mix)
    u = rmsnorm(x, norm_pre_ffn)
    g, up = _split_cols(jnp.einsum('btd,df->btf', u, w_gate_up), (D_FF, D_FF))
    f = jnp.einsum('btf,fd->btd', jax.nn.silu(g) * up, w_down)
    x = x + rmsnorm(f, norm_post_ffn)
    return x, new_st

def setup_inputs(seed: int = 0) -> dict:
    key = jax.random.key(seed)
    ks = jax.random.split(key, 32)
    f32 = jnp.float32
    nrm = lambda k, shape, s: jax.random.normal(k, shape, f32) * s
    gain = lambda k, shape: 1.0 + 0.05 * jax.random.normal(k, shape, f32)
    dt = jnp.exp(jax.random.uniform(ks[20], (DEPTH, GDN_HEADS), f32, np.log(1e-3), np.log(1e-1)))
    return {
        "x_prompt": nrm(ks[0], (BATCH, SEQ, D_MODEL), 1.0),
        "x_sample": nrm(ks[1], (DEC_BATCH, DEC_SEQ, D_MODEL), 1.0),
        "state_mlstm_C": nrm(ks[2], (DEPTH, DEC_BATCH, MLSTM_HEADS, HEAD_DIM, HEAD_DIM), 0.1),
        "state_mlstm_n": nrm(ks[3], (DEPTH, DEC_BATCH, MLSTM_HEADS, HEAD_DIM), 0.5),
        "state_mlstm_m": 2.0 + nrm(ks[4], (DEPTH, DEC_BATCH, MLSTM_HEADS), 1.0),
        "state_gdn_S": nrm(ks[5], (DEPTH, DEC_BATCH, GDN_HEADS, HEAD_DIM, HEAD_DIM), 0.05),
        "state_gdn_conv": nrm(ks[6], (DEPTH, DEC_BATCH, CONV_W - 1, 3 * GDN_WIDTH), 0.5),
        "meta_tokens": nrm(ks[7], (N_META, D_MODEL), 1.0),
        "norm_pre_mix": gain(ks[8], (DEPTH, D_MODEL)),
        "norm_post_mix": gain(ks[9], (DEPTH, D_MODEL)),
        "norm_pre_ffn": gain(ks[10], (DEPTH, D_MODEL)),
        "norm_post_ffn": gain(ks[11], (DEPTH, D_MODEL)),
        "w_in": nrm(ks[12], (DEPTH, D_MODEL, IN_COLS), D_MODEL ** -0.5),
        "mlstm_b_i": nrm(ks[13], (DEPTH, MLSTM_HEADS), 0.1),
        "mlstm_b_f": 3.0 + nrm(ks[14], (DEPTH, MLSTM_HEADS), 0.5),
        "mlstm_norm": gain(ks[15], (DEPTH, MLSTM_HEADS, HEAD_DIM)),
        "gdn_conv_w": nrm(ks[16], (DEPTH, CONV_W, 3 * GDN_WIDTH), CONV_W ** -0.5),
        "gdn_A_log": jnp.log(jax.random.uniform(ks[17], (DEPTH, GDN_HEADS), f32, 1.0, 16.0)),
        "gdn_dt_bias": jnp.log(jnp.expm1(dt)),
        "gdn_norm": gain(ks[18], (DEPTH, GDN_HEADS, HEAD_DIM)),
        "w_out": nrm(ks[19], (DEPTH, MIX_WIDTH, D_MODEL), MIX_WIDTH ** -0.5),
        "w_gate_up": nrm(ks[21], (DEPTH, D_MODEL, 2 * D_FF), D_MODEL ** -0.5),
        "w_down": nrm(ks[22], (DEPTH, D_FF, D_MODEL), D_FF ** -0.5),
    }

def reference(x_prompt, x_sample, state_mlstm_C, state_mlstm_n, state_mlstm_m, state_gdn_S, state_gdn_conv,
              meta_tokens, norm_pre_mix, norm_post_mix, norm_pre_ffn, norm_post_ffn, w_in, mlstm_b_i, mlstm_b_f,
              mlstm_norm, gdn_conv_w, gdn_A_log, gdn_dt_bias, gdn_norm, w_out, w_gate_up, w_down):
    f32 = jnp.float32
    B = x_prompt.shape[0]
    Bs = x_sample.shape[0]
    xp = jnp.concatenate([jnp.broadcast_to(meta_tokens.astype(x_prompt.dtype)[None], (B, N_META, D_MODEL)), x_prompt], axis=1)
    xs = x_sample
    p_states, s_states = [], []
    for l in range(DEPTH):
        w = (norm_pre_mix[l], norm_post_mix[l], norm_pre_ffn[l], norm_post_ffn[l], w_in[l], mlstm_b_i[l],
             mlstm_b_f[l], mlstm_norm[l], gdn_conv_w[l], gdn_A_log[l], gdn_dt_bias[l], gdn_norm[l], w_out[l],
             w_gate_up[l], w_down[l])
        st_p = (jnp.zeros((B, MLSTM_HEADS, HEAD_DIM, HEAD_DIM), f32),
                jnp.zeros((B, MLSTM_HEADS, HEAD_DIM), f32),
                jnp.zeros((B, MLSTM_HEADS), f32),
                jnp.zeros((B, GDN_HEADS, HEAD_DIM, HEAD_DIM), f32),
                jnp.zeros((B, CONV_W - 1, 3 * GDN_WIDTH), f32))
        xp, new_p = decoder_layer(xp, st_p, *w, lead=N_META, chunk=CHUNK)
        st_s = (state_mlstm_C[l].astype(f32), state_mlstm_n[l].astype(f32), state_mlstm_m[l].astype(f32),
                state_gdn_S[l].astype(f32), state_gdn_conv[l].astype(f32))
        xs, new_s = decoder_layer(xs, st_s, *w, lead=0, chunk=xs.shape[1])
        p_states.append(new_p)
        s_states.append(new_s)
    y_prompt = xp[:, N_META:]
    y_sample = xs
    pC, pn, pm, pS, pconv = [jnp.stack([s[i] for s in p_states]) for i in range(5)]
    sC, sn, sm, sS, sconv = [jnp.stack([s[i] for s in s_states]) for i in range(5)]
    return (y_prompt, y_sample, pC, pn, pm, pS, pconv, sC, sn, sm, sS, sconv)


_drawn_inputs = setup_inputs


def setup_inputs(seed=0):
    import zlib

    import numpy as np

    out = dict(_drawn_inputs(seed))
    spreads = {}
    factors = {}
    for name, (base, spread) in spreads.items():
        noise = np.random.default_rng([zlib.crc32(name.encode()), seed]).standard_normal(out[name].shape)
        drawn = base * np.exp(spread * noise) if base else spread * noise
        out[name] = __import__('jax').numpy.asarray(drawn.astype(out[name].dtype))
    for name, factor in factors.items():
        out[name] = (out[name] * factor).astype(out[name].dtype)
    return out
```

```python
from contextlib import ExitStack

import numpy as np

import concourse.bass as bass
from concourse import mybir

F32 = mybir.dt.float32
F32R = mybir.dt.float32r
U8 = mybir.dt.uint8
ALU = mybir.AluOpType
ACT = mybir.ActivationFunctionType

P = 128
D = 2048
KT = D // P
H = 8
NB, DEC = 8, 4
META, SEQ = 16, 256
NP = META + SEQ
T = NP + NB * DEC
TP = 384
T2 = T - 2 * P
P2 = NP - 2 * P
NG = NB + 1
W1 = H * P
IN_COLS = 8 * W1 + 4 * H
GDN_COL = 4 * W1 + 2 * H
FF = 5632
FG = FF // 512
TAPS = 4
DEC0 = NP + TAPS - 1
GW = DEC + TAPS - 1
XW = DEC0 + NB * GW
YW = XW - (TAPS - 1)
EPS = 1e-6
QS = float(P) ** -0.5
NEG = -1e30
EXP_LN_SET = 6
LEVELS = 7
TILE = [(0, 0, P), (1, P, P), (2, 2 * P, T2)]


def constant_tables():
    pos = np.arange(TP)
    group = np.where(pos < NP, NB, (pos - NP) // DEC)
    group[T:] = 99
    j = np.arange(P)
    cols = {}
    cols["ident"] = np.eye(P)
    cols["ones"] = np.ones((P, P))
    cols["mean"] = np.full((P, P), 1.0 / P)

    def cap(tile, toks):
        a = tile * P + j
        ok = (toks[None, :] >= a[:, None]) & (group[toks][None, :] == group[a][:, None]) & (a[:, None] < T)
        return np.where(ok, 0.0, NEG)
    cols["cap_g"] = np.concatenate([cap(t, np.arange(s, s + n)) for t, s, n in TILE], 1)
    cols["cap_m"] = np.concatenate([cap(0, np.arange(NP)), cap(1, np.arange(P, NP)), cap(2, np.arange(2 * P, T))], 1)
    cols["neg_strict"] = -np.concatenate([1.0 - np.eye(P)[:, :n] for _, _, n in TILE], 1)
    g2 = group[2 * P + j]
    cols["gmask"] = (g2[:, None] == np.arange(NG)[None, :]) * 1.0
    cols["gmask_rows"] = np.broadcast_to((np.arange(NG)[:, None] == g2[None, :T2]).reshape(-1) * 1.0, (P, NG * T2))
    at, out = {}, []
    n = 0
    for k, v in cols.items():
        at[k] = (n, n + v.shape[1])
        n += v.shape[1]
        out.append(v)
    joins = []
    for lower in (True, False):
        for lv in range(LEVELS):
            s = 1 << lv
            r, c = j[:, None], j[None, :]
            m = (r // (2 * s) == c // (2 * s)) & (r // s % 2 == 1) & (c // s % 2 == 0)
            m = m if lower else m.T
            joins.append(np.concatenate([m[:, :n] for _, _, n in TILE], 1))
    start = np.zeros(T)
    start[0] = 1
    start[NP::DEC] = 1
    chunk = start.copy()
    chunk[[P, 2 * P]] = 1
    scan = np.stack([np.broadcast_to(1 - start, (H, T)), np.broadcast_to(1 - chunk, (H, T))], 1)
    return (np.concatenate(out, 1).astype(np.float32), at, np.stack(joins, 1).astype(np.float32),
            np.ascontiguousarray(scan).astype(np.float32))


_, CONST_AT, _, _ = constant_tables()
CONST_W = max(b for _, b in CONST_AT.values())


class Steps:

    def __init__(self, sem, names):
        self.sem, self.names, self.done = sem, names.split(), 0
        self.n = len(self.names)

    def at(self, it, name):
        return it * self.n + (self.n + self.names.index(name) + 1)

    def before(self, it, name):
        return it * self.n + (self.n + self.names.index(name))

    def prev(self, it, name):
        return it * self.n + (self.names.index(name) + 1)

    def skip(self, eng, it, names):
        eng.wait_ge(self.sem, self.before(it, names[0]))
        eng.sem_inc(self.sem, len(names))
        for name in names:
            self.step(name)

    def step(self, name):
        assert self.names[self.done % self.n] == name, (name, self.names[self.done % self.n])
        self.done += 1
        return self.sem, 1


def build_layer(nc, A, O):
    with ExitStack() as ctx:
        ctx.enter_context(nc.allow_non_contiguous_dma(reason="a few short columns"))

        def sb(name, shape, dt=F32, c=ctx):
            return c.enter_context(nc.sbuf_tensor(name, shape, dt))

        def sem(name):
            return ctx.enter_context(nc.semaphore(name))

        x_spill = nc.dram_tensor("x_spill", (P, KT, T), F32, kind="Internal").ap()

        raw = sb("raw", [P, 2, KT, P])
        whi = [sb(f"whi{i}", [P, KT, P], F32R) for i in range(2)]
        wlo = [sb(f"wlo{i}", [P, KT, P], F32R) for i in range(2)]
        u_hi, u_lo = sb("u_hi", [P, KT, T], F32R), sb("u_lo", [P, KT, T], F32R)
        first = ExitStack()
        join_masks = sb("join_masks", [P, 2 * LEVELS, T], F32, first)
        first.close()
        mix_hi, mix_lo = sb("mix_hi", [P, KT, T], F32R), sb("mix_lo", [P, KT, T], F32R)
        cst = sb("cst", [P, CONST_W])
        joins = sb("joins", [P, 2 * LEVELS, T], U8)
        norms = sb("norms", [P, 80])
        eps_c = sb("eps_c", [P, 3])
        sel = sb("sel", [H, P])
        rows_m = sb("rows_m", [H, 2 * T + NB * DEC])
        rows_g = sb("rows_g", [H, 3 * T])
        m8 = sb("m8", [H, NB])
        bias8 = sb("bias8", [H, 4])
        mp = sb("mp", [H, NB])
        decay = sb("decay", [H, 1])
        ssum = sb("ssum", [P, 4])
        cols = sb("cols", [P, 3, 6, H])

        def C(name, rows=P):
            a, b = CONST_AT[name]
            return cst[0:rows, a:b]
        ident, ones, mean = C("ident"), C("ones"), C("mean")

        mixers = ExitStack()
        m_ = lambda name, shape, dt=F32: sb(name, shape, dt, mixers)
        stage = m_("stage", [P, 3, XW])
        stage_z = m_("stage_z", [P, T])
        convw = m_("convw", [P, 96])
        conv_in = m_("conv_in", [P, 3, H, NB * 3])
        conv_out = m_("conv_out", [P, 3, H, NG * 3])
        n_in = m_("n_in", [P, NB * H])
        n_out = m_("n_out", [P, NG, H])
        st_in = m_("st_in", [P, NB, P])
        st_out = m_("st_out", [P, NG, P])
        vm = m_("vm", [T2, NG, P])
        kn = m_("kn", [P, TP])
        qn = m_("qn", [P, T])
        dec = m_("dec", [P, T])
        k_tok = m_("k_tok", [P, 3, P])
        v_tok = m_("v_tok", [P, 3, P])
        fac = m_("fac", [P, T])
        gate = m_("gate", [P, T])
        mixf = m_("mixf", [P, T])
        sq = m_("sq", [P, 2, T])
        dcs = m_("dcs", [P, 2 + NB])
        only_g = ExitStack()
        g_ = lambda name, shape, dt=F32: sb(name, shape, dt, only_g)
        y = g_("y", [P, 3, YW])
        cs = g_("cs", [P, 3, TP])
        kb = g_("kb", [P, T])
        qeg = g_("qeg", [P, T])
        decn = g_("decn", [P, T])
        nat = g_("nat", [P, TP])
        pb = g_("pb", [P, TP])
        tinv, uinv = g_("tinv", [P, 3, P]), g_("uinv", [P, 3, P])
        kh_tok = g_("kh_tok", [P, 3, P])
        nkd = g_("nkd", [P, T])
        nkdm = g_("nkdm", [P, NG, T2])
        wv = g_("wv", [P, 3, P])
        s_chunk = g_("s_chunk", [P, 2, P])
        only_g.close()
        only_m = ExitStack()
        n_ = lambda name, shape, dt=F32: sb(name, shape, dt, only_m)
        sc_e = n_("sc_e", [P, 464])
        sc_p = n_("sc_p", [P, 464])
        vpad = n_("vpad", [P, TP])
        qi = n_("qi", [P, NB * DEC])
        nq = n_("nq", [P, NB * DEC])
        nm = n_("nm", [P, NB])
        hm = n_("hm", [P, T])
        only_m.close()

        x_c = ExitStack()
        x_ = lambda name, shape, dt=F32: sb(name, shape, dt, x_c)
        xtok = x_("xtok", [P, 3, D])
        x_out = x_("x_out", [P, 2, T])
        x_c.close()
        row_c = ExitStack()
        r_ = lambda name, shape, dt=F32: sb(name, shape, dt, row_c)
        gates = r_("gates", [4 * H, T])
        yf = r_("yf", [H, 2, T])
        la = r_("la", [H, 2, T])
        scan_m = r_("scan_m", [H, 2, T])
        li = r_("li", [H, T])
        b_row = r_("b_row", [H, T])
        m_row = r_("m_row", [H, T])
        col_src = r_("col_src", [H, 6, TP])
        row_c.close()
        tail_c = ExitStack()
        conv_back = sb("conv_back", [NG * 3, 3 * W1], F32, tail_c)
        tail_c.close()
        mixers.close()
        ffn = ExitStack()
        f_ = lambda name, shape, dt=F32: sb(name, shape, dt, ffn)
        x2 = f_("x2", [P, KT, T])
        acc_s = f_("acc_s", [P, KT, T])
        squares = ExitStack()
        fs16 = sb("fs16", [P, KT, T], F32, squares)
        squares.close()
        h_hi, h_lo = f_("h_hi", [P, 2, 4, T], F32R), f_("h_lo", [P, 2, 4, T], F32R)
        fe, fh, frb = f_("fe", [P, T]), f_("fh", [P, T]), f_("frb", [P, T])
        fsq = f_("fsq", [P, 2, T])
        ffn.close()

        conv_rows = [vm[0:NB * 3].rearrange("p g e -> p (g e)")[:, 0:W1],
                     st_out[0:NB * 3].rearrange("p g e -> p (g e)")[:, 0:W1],
                     st_in[0:NB * 3].rearrange("p g e -> p (g e)")[:, 0:W1]]
        norm_rows = k_tok[0:80, 0, :]
        tap_rows = k_tok[0:96, 1, :]
        n_rows = k_tok[0:NB * H, 2, :]

        psum = ctx.enter_context(nc.psum_tensor("psum", [P, 8, 512], F32))

        def B(i, a=0, b=T):
            return psum[:, 2 + i, a:b]

        raw_in = [sem("raw_in0"), sem("raw_in1")]
        hi_done, lo_done = sem("hi_done"), sem("lo_done")
        lo_pool = sem("lo_pool")
        unit_done = sem("unit_done")
        evac_done = sem("evac_done")
        const_in, small_in, x_in, conv_rows_in = sem("const_in"), sem("small_in"), [sem(f"x_in{t}") for t in range(3)], sem("conv_rows_in")
        gates_in = sem("gates_in")
        spill_done = [sem("spill_done0"), sem("spill_done1")]
        m_out = sem("m_out")
        pads_ready = sem("pads_ready")
        st_loaded, st_stored = sem("st_loaded"), sem("st_stored")
        x_back, rows_out, y_out = sem("x_back"), sem("rows_out"), [sem("y_out0"), sem("y_out1")]
        rows_in, joins_in = sem("rows_in"), sem("joins_in")
        acc_zero = sem("acc_zero")
        join_turn = sem("join_turn")
        tail = Steps(sem("tail"), "c0 c1 c2 c3 c4 c5 n")
        tail_v = Steps(sem("tail_v"), "c0 c1 c2 c3 c4 c5 n")
        y_tok = raw[:, :, 0:12, :].rearrange("p b (t k) n -> p b t k n", t=3)

        U_G, U_M = 4, 4 + 4 * H
        U_O = U_M + 4 * H
        U_F = U_O + KT
        U_END = U_F + 12 * FG

        g_pe = Steps(sem("g_pe"), "bc ss kk tr l0 " + " ".join(f"p{i} q{i}" for i in range(1, LEVELS))
                     + " nkd w0 s1 w1 s2 w2 o st ms")
        g_act = Steps(sem("g_act"), "ln rs dec_exp vb0 vb1 vb2 z0 z1 z2 p1 p2 p3 e0p e0d e0l e0s p4 p5 p6 e1p e1d e1l e1s"
                      + " nkd w0 w1 w2 osq e2p e2d e2l e2s oln ors esq mixhi")
        g_dve = Steps(sem("g_dve"), "qn kn kb qeg d1 d2 d3 e0 e1 e2 qkd nat kb0 kb1 kb2 kh0 kh1 kh2 gate "
                      + "t0 u0 t1 u1 c0w0 c0w1 t2 u2 c0w2 c0w3 t3 u3 t4 u4 c1w0 c1w1 t5 u5 c1w2 c1w3 t6 u6"
                      + " nkdm s1 s2 c2w0 c2w1 c2w2 c2w3 so0 so1 sp cs_p cs_d omul omix mixlo")
        g_pool = Steps(sem("g_pool"), "sel decn ti ui sdec save_p save_d wm")
        m_pe = Steps(sem("m_pe"), "bc tr sc num den st ms")
        m_act = Steps(sem("m_act"), "q k vp oe v exp absd hsq ln rs mixhi")
        m_dve = Steps(sem("m_dve"), "o1 gate e0 e1 e2 kw0 kw1 kw2 pm qi nq dcp dmax drec h nm na np co0 co1 cp fg mixf mixlo")
        m_pool = Steps(sem("m_pool"), "sel vm cdec")
        o_pe, o_act = Steps(sem("o_pe"), "ms"), Steps(sem("o_act"), "copy sq")
        f_act, f_dve = Steps(sem("f_act"), "e hi"), Steps(sem("f_dve"), "add rec s h lo")
        added = Steps(sem("added"), "0 1 2 3")
        each = lambda *names: " ".join(f"{x}{k}" for k in range(KT) for x in names)
        a_pe = Steps(sem("a_pe"), "norms rb " + each("x") + " sel cols conv")
        a_act = Steps(sem("a_act"), "ss0 ss1 ss2 ln r " + each("xo", "uh") + " gates ea bexp abs aexp aln iexp em eg wl kh " + " ".join(f"e{c}{x}" for c in range(3) for x in "pdls") + " esq")
        a_dve = Steps(sem("a_dve"), "ones norms convw n_in dg0 dg1 dg2 rb " + each("ut", "ul")
                      + " li yf0 yf1 b1 b2 lf sp lg bsc gsc c mx0 t8 mx1 ng0 ng1 msc r it wl0 wl1 ngg kh0 kh1 kh2 kh3 nb bc cols ci0 ci1 " + " ".join(f"c{c}w{i}" for c in range(3) for i in range(TAPS)) + " cs_p cs_d")
        a_pool = Steps(sem("a_pool"), "z0 z1 z2 z3 z4 z5 joins")
        n_pe = Steps(sem("n_pe"), "ms2 ffn " + each("y"))
        n_act = Steps(sem("n_act"), "ln r " + each("sq") + " ln2 r2 " + each("uh") + " " + each("fq") + " ln3 r3 " + each("yc"))
        n_dve = Steps(sem("n_dve"), each("t", "x") + " " + each("ut", "ul") + " " + each("ft", "fx"))


        class Unit:
            def __init__(self, base, it, i, per=4):
                self.u = base + per * it + i
                self.landed = 16 * ((base + i) // 2 - 1) + 8 * per * it
                self.slot = i % 2

        w_in_v = A["w_in"][0].rearrange("(k p) n -> p k n", p=P)
        w_out_v = A["w_out"][0].rearrange("(k p) n -> p k n", p=P)
        w_gu_v = A["w_gate_up"][0].rearrange("(k p) n -> p k n", p=P)
        w_dn_v = A["w_down"][0].rearrange("(k p) n -> p k n", p=P)

        def load_unit(eng, w, view, split=lo_done):
            eng.wait_ge(split, w.u - 2)
            dst = raw[:, w.slot]
            if view.shape[1] == 4:
                dst = dst.rearrange("p (k m) n -> p k (m n)", k=4)
            eng.dma_start(dst, view).then_inc(raw_in[w.slot], 16)

        def split_hi(act, w):
            act.wait_ge(raw_in[w.slot], w.landed)
            act.wait_ge(unit_done, w.u - 2)
            act.activation(whi[w.slot][:, :, :], raw[:, w.slot], ACT.Copy).then_inc(hi_done, 1)

        def split_lo(eng, w, done=lo_done):
            eng.wait_ge(hi_done, w.u)
            eng.tensor_tensor(wlo[w.slot][:, :, :], raw[:, w.slot], whi[w.slot][:, :, :].bitcast(F32),
                              ALU.subtract).then_inc(done, 1)

        def products(pe, out, pairs, first, last):
            for n, (a, b, xh, xl) in enumerate(pairs):
                pe.matmul(out, a, xh, start=(first and n == 0), stop=False)
                pe.matmul(out, a, xl, start=False, stop=False)
                ins = pe.matmul(out, b, xh, start=False, stop=(last and n == len(pairs) - 1))
            return ins

        def tiles(w, kts, xh, xl):
            return [(whi[w.slot][:, k, :], wlo[w.slot][:, k, :], xh[:, k, :], xl[:, k, :]) for k in kts]

        PARTS = 8

        def unit_part(pe, w, part, xh, xl, split=lo_pool):
            if part == 0:
                pe.wait_ge(split, w.u)
                pe.wait_ge(evac_done, w.u - 2)
            n = KT // PARTS
            ins = products(pe, psum[:, w.slot, 0:T], tiles(w, range(part * n, part * n + n), xh, xl),
                           first=(part == 0), last=(part == PARTS - 1))
            if part == PARTS - 1:
                ins.then_inc(unit_done, 1)

        SLOT_G = dict(bc=0, ss=1)
        for n, name in enumerate(g_pe.names[2:]):
            SLOT_G[name] = min(4 * PARTS, 6 + n + (n > 21))
        SLOT_M = dict(bc=1, tr=3, sc=5, num=11, den=13, st=16, ms=22)

        def group_cols(t, a=NP, w=DEC):
            return t[:, a:a + NB * w].rearrange("p (b w) -> p b w", w=w)

        def conv_groups(t):
            t = t[:, DEC0:DEC0 + (NB - 1) * GW + DEC]
            return bass.AP(t.tensor, t.offset, [list(t.ap[0]), [GW, NB], [1, DEC]])

        def stage_dst(i, kind):
            if i == 3:
                return [(stage_z[:, :], (0, T))]
            if kind == "m":
                return [(stage[:, i, 0:T], (0, T))]
            return [(stage[:, i, TAPS - 1:DEC0], (0, NP)),
                    (stage[:, i, DEC0:XW].rearrange("p (b w) -> p b w", w=GW)[:, :, TAPS - 1:GW], (NP, T))]

        def evacuate(act, w, i, kind):
            act.wait_ge(unit_done, w.u)
            dst = stage_dst(i, kind)
            for n, (out, (a, b)) in enumerate(dst):
                src = psum[:, w.slot, a:b]
                if len(out.shape) == 3:
                    src = src.rearrange("p (b w) -> p b w", w=DEC)
                ins = act.activation(out, src, ACT.Copy)
                if n == len(dst) - 1:
                    ins.then_inc(evac_done, 1)

        block = ctx.enter_context(nc.Block())

        @block.sync
        def _(sp):
            xp, xs, meta = A["x_prompt"][0], A["x_sample"].rearrange("b t d -> (b t) d"), A["meta_tokens"]
            sp.dma_start(xtok[0:META, 0, :], meta).then_inc(x_in[0], 16)
            sp.dma_start(xtok[META:P, 0, :], xp[0:P - META, :]).then_inc(x_in[0], 16)
            sp.dma_start(xtok[:, 1, :], xp[P - META:2 * P - META, :]).then_inc(x_in[1], 16)
            sp.dma_start(xtok[0:P2, 2, :], xp[2 * P - META:SEQ, :]).then_inc(x_in[2], 16)
            sp.dma_start(xtok[P2:T2, 2, :], xs).then_inc(x_in[2], 16)
            sp.dma_start(raw[:, 1, :, 0:2 * H], w_in_v[:, :, 4 * W1:4 * W1 + 2 * H]).then_inc(gates_in, 16)
            sp.dma_start(raw[:, 1, :, 2 * H:4 * H], w_in_v[:, :, IN_COLS - 2 * H:IN_COLS]).then_inc(gates_in, 16)

            def head_units(base, col, it, split):
                for i in range(4):
                    load_unit(sp, Unit(base, it, i), w_in_v[:, :, bass.ds(col + i * W1 + it * P, P)], split(i))

            def out_units(it, split):
                for i in range(4):
                    load_unit(sp, Unit(U_O, it, i), w_out_v[:, :, bass.ds((4 * it + i) * P, P)], split(i))
            head_units(U_G, GDN_COL, 0, lambda i: lo_done)
            head_units(U_G, GDN_COL, 1, lambda i: lo_done if i < 2 else lo_pool)
            with sp.Fori(2, H) as it:
                head_units(U_G, GDN_COL, it, lambda i: lo_pool)
            with sp.Fori(0, H) as it:
                head_units(U_M, 0, it, lambda i: lo_pool)
            out_units(0, lambda i: lo_pool if i < 3 else lo_done)
            with sp.Fori(1, KT // 4) as it:
                out_units(it, lambda i: lo_done)

            def gate_up(group, base, it, i0, per=24):
                for j in range(4):
                    for half in range(2):
                        load_unit(sp, Unit(base, it, i0 + 2 * j + half, per),
                                  w_gu_v[:, :, bass.ds(half * FF + group * 512 + j * P, P)])

            def down(group, base, it, i0, per=24):
                for n in range(4):
                    load_unit(sp, Unit(base, it, i0 + n, per),
                              w_dn_v[:, bass.ds(4 * group, 4), n * 512:n * 512 + 512])
            gate_up(0, U_F, 0, 0)
            with sp.Fori(0, FG // 2) as it:
                gate_up(2 * it + 1, U_F + 8, it, 0)
                down(2 * it, U_F + 8, it, 8)
                gate_up(2 * it + 2, U_F + 8, it, 12)
                down(2 * it + 1, U_F + 8, it, 20)
            down(FG - 1, U_END - 4, 0, 0)
            for g in range(KT // 4):
                b, c = g % 2, slice(512 * g, 512 * g + 512)
                sp.wait_ge(n_act.sem, n_act.at(0, f"yc{4 * g + 3}"))
                yp, ys = O["y_p"][0], O["y_s"].rearrange("b t d -> (b t) d")
                for rows, t, dst in ((slice(META, P), 0, yp[0:P - META, c]), (slice(0, P), 1, yp[P - META:2 * P - META, c]),
                                     (slice(0, P2), 2, yp[2 * P - META:SEQ, c]), (slice(P2, T2), 2, ys[:, c])):
                    sp.dma_start(dst, y_tok[rows, b, t, :, :].rearrange("p k n -> p (k n)")).then_inc(y_out[b], 16)
            for b in range(2):
                sp.wait_ge(y_out[b], 64 * (KT // 8))

        @block.gpsimd
        def _(pool):
            for c in (a_pool, g_pool, m_pool):
                pool.sem_inc(c.sem, c.n)
            pool.sem_inc(lo_pool, U_G + 3)
            for n, part in enumerate((stage[:, :, 0:TAPS - 1], kn[:, T:TP])):
                pool.memset(part, 0.0).then_inc(*a_pool.step(f"z{n}"))
            for k in range(KT):
                pool.wait_ge(a_act.sem, a_act.at(0, f"xo{k}"))
                pool.dma_start(x_spill[:, k, :], x_out[:, k % 2, :]).then_inc(spill_done[k % 2], 16)
            pool.memset(col_src[:, :, :], 0.0).then_inc(*a_pool.step("z2"))
            pool.dma_start(scan_m[:, :, :], A["scan_mask"]).then_inc(st_stored, 16)
            pool.wait_ge(a_dve.sem, a_dve.at(0, "ci1"))
            pool.wait_ge(a_act.sem, a_act.at(0, "kh"))
            for n, part in enumerate((cs[:, :, T:TP], nat[:, T:TP], pb[:, T:TP])):
                pool.memset(part, 0.0).then_inc(*a_pool.step(f"z{3 + n}"))
            pool.wait_ge(joins_in, 16)
            pool.tensor_copy(joins[:, :, :], join_masks[:, :, :]).then_inc(*a_pool.step("joins"))
            pool.dma_start(O["p_m"].rearrange("l b h -> h (l b)"), m_row[:, NP - 1:NP]).then_inc(m_out, 16)
            pool.dma_start(O["s_m"][0].rearrange("b h -> h b"), group_cols(m_row)[:, :, DEC - 1]).then_inc(m_out, 16)

            def pads(h):
                pool.wait_ge(const_in, 16)
                pool.tensor_copy(stage[:, :, DEC0:XW].rearrange("p c (b w) -> p c b w", w=GW)[:, :, :, 0:TAPS - 1],
                                 conv_in[:, :, bass.ds(h, 1), :].rearrange("p c o (b r) -> p (c o) b r", r=3)
                                 ).then_inc(pads_ready, 1)
            pads(0)
            C_v = A["state_mlstm_C"][0].rearrange("b h d e -> h d b e")
            S_v = A["state_gdn_S"][0].rearrange("b h d e -> h d b e")
            CO_s, CO_p = O["s_C"][0].rearrange("b h d e -> h d b e"), O["p_C"][0].rearrange("b h d e -> h d b e")
            SO_s, SO_p = O["s_S"][0].rearrange("b h d e -> h d b e"), O["p_S"][0].rearrange("b h d e -> h d b e")

            def of(view, h):
                return view[bass.ds(h, 1)].rearrange("h d b e -> d (h b) e")

            def load_state(view, h):
                pool.dma_start(st_in[:, :, :], of(view, h)).then_inc(st_loaded, 16)

            def store_state(s_view, p_view, h):
                pool.dma_start(of(s_view, h), st_out[:, 0:NB, :]).then_inc(st_stored, 16)
                pool.dma_start(of(p_view, h), st_out[:, NB:NG, :]).then_inc(st_stored, 16)
            load_state(S_v, 0)
            pool.wait_ge(a_dve.sem, a_dve.at(0, "c2w3"))
            pool.wait_ge(m_out, 32)

            split_lo(pool, Unit(U_G, 0, 4), lo_pool)

            def gdn(it, last):
                nxt = [Unit(U_G, it, 4 + i) for i in range(5)]
                pool.wait_ge(g_pe.sem, g_pe.before(it, "bc"))
                pool.wait_ge(const_in, 16)
                pool.tensor_copy(sel[:, :], ident[0:H, bass.ds(it, 1)].to_broadcast([H, P])).then_inc(*g_pool.step("sel"))
                if not last:
                    pool.wait_ge(g_dve.sem, g_dve.prev(it, "c2w3"))
                    pads(it + 1)
                split_lo(pool, nxt[1], lo_pool)
                pool.wait_ge(g_act.sem, g_act.at(it, "dec_exp"))
                pool.wait_ge(g_dve.sem, g_dve.before(it, "qn"))
                pool.tensor_tensor(decn[:, :], dec[:, :], C("neg_strict"), ALU.mult).then_inc(*g_pool.step("decn"))
                for name, buf in (("ti", tinv), ("ui", uinv)):
                    pool.tensor_tensor(buf[:, :, :], ident.unsqueeze(1).to_broadcast([P, 3, P]),
                                       ident.unsqueeze(1).to_broadcast([P, 3, P]), ALU.mult).then_inc(*g_pool.step(name))
                pool.wait_ge(st_loaded, 16 * (it + 1))
                pool.wait_ge(g_dve.sem, g_dve.at(it, "d3"))
                pool.wait_ge(st_stored, 32 * it + 16)
                pool.tensor_tensor(st_out[:, 0:NB, :], st_in[:, :, :],
                                   dcs[:, 2:2 + NB].unsqueeze(2).to_broadcast([P, NB, P]), ALU.mult
                                   ).then_inc(*g_pool.step("sdec"))
                pool.wait_ge(evac_done, Unit(U_G, it, 2).u)
                pool.wait_ge(const_in, 16)
                pool.tensor_copy(conv_out[:, :, bass.ds(it, 1), 3 * NB:].rearrange("p c o r -> p (c o) r"),
                                 stage[:, :, DEC0 - 3:DEC0]).then_inc(*g_pool.step("save_p"))
                pool.wait_ge(const_in, 16)
                pool.tensor_copy(conv_out[:, :, bass.ds(it, 1), 0:3 * NB].rearrange("p c o (b r) -> p (c o) b r", r=3),
                                 stage[:, :, DEC0:XW].rearrange("p c (b w) -> p c b w", w=GW)[:, :, :, GW - 3:GW]
                                 ).then_inc(*g_pool.step("save_d"))
                split_lo(pool, nxt[2], lo_pool)
                split_lo(pool, nxt[3], lo_pool)
                pool.wait_ge(g_act.sem, g_act.at(it, "w2"))
                pool.tensor_tensor(vm[:, :, :], wv[0:T2, 2, :].unsqueeze(1).to_broadcast([T2, NG, P]),
                                   C("gmask", T2).unsqueeze(2).to_broadcast([T2, NG, P]), ALU.mult
                                   ).then_inc(*g_pool.step("wm"))
                split_lo(pool, nxt[4], lo_pool)
                pool.wait_ge(g_pe.sem, g_pe.at(it, "o"))
                pool.wait_ge(g_pool.sem, g_pool.at(it, "sdec"))
                load_state(C_v, 0) if last else load_state(S_v, it + 1)
                pool.wait_ge(g_dve.sem, g_dve.at(it, "sp"))
                store_state(SO_s, SO_p, it)
            with pool.Fori(0, H - 1) as it:
                gdn(it, False)
            gdn(H - 1, True)
            pool.wait_ge(g_dve.sem, g_dve.at(H - 1, "mixlo"))
            pool.memset(vpad[:, T:TP], 0.0).then_inc(pads_ready, 1)

            def mlstm(it, last):
                split = (lambda i: None) if last else (lambda i: split_lo(pool, Unit(U_M, it, 4 + i), lo_pool))
                pool.wait_ge(m_pe.sem, m_pe.before(it, "bc"))
                pool.wait_ge(const_in, 16)
                pool.tensor_copy(sel[:, :], ident[0:H, bass.ds(it, 1)].to_broadcast([H, P])).then_inc(*m_pool.step("sel"))
                split(1)
                pool.wait_ge(m_act.sem, m_act.at(it, "v"))
                pool.wait_ge(m_pe.sem, m_pe.before(it, "bc"))
                pool.tensor_tensor(vm[:, :, :], v_tok[0:T2, 2, :].unsqueeze(1).to_broadcast([T2, NG, P]),
                                   C("gmask", T2).unsqueeze(2).to_broadcast([T2, NG, P]), ALU.mult
                                   ).then_inc(*m_pool.step("vm"))
                split(2)
                pool.wait_ge(st_loaded, 16 * (it + H + 1))
                pool.wait_ge(m_dve.sem, m_dve.at(it, "dcp"))
                pool.wait_ge(st_stored, 32 * it + 32 * H + 16)
                pool.tensor_tensor(st_out[:, 0:NB, :], st_in[:, :, :],
                                   dcs[:, 0:NB].unsqueeze(2).to_broadcast([P, NB, P]), ALU.mult
                                   ).then_inc(*m_pool.step("cdec"))
                split(3)
                if not last:
                    pool.wait_ge(m_pe.sem, m_pe.at(it, "num"))
                    pool.wait_ge(m_pool.sem, m_pool.at(it, "cdec"))
                    load_state(C_v, it + 1)
                pool.wait_ge(m_dve.sem, m_dve.at(it, "cp"))
                store_state(CO_s, CO_p, it)
                split(4)
            with pool.Fori(0, H - 1) as it:
                mlstm(it, False)
            mlstm(H - 1, True)
            pool.wait_ge(tail_v.sem, tail_v.at(0, "c5"))
            pool.dma_start(O["s_conv"][0].rearrange("b r n -> (b r) n"), conv_back[0:3 * NB, :]).then_inc(rows_out, 16)
            pool.dma_start(O["p_conv"][0, 0], conv_back[3 * NB:3 * NG, :]).then_inc(rows_out, 16)
            pool.wait_ge(tail_v.sem, tail_v.at(0, "n"))
            pool.dma_start(O["s_n"][0].rearrange("b h d -> (b h) d"), k_tok[0:NB * H, 0, :]).then_inc(rows_out, 16)
            pool.dma_start(O["p_n"][0, 0], k_tok[NB * H:NG * H, 0, :]).then_inc(rows_out, 16)
            pool.wait_ge(st_stored, 64 * H + 16)
            pool.wait_ge(rows_out, 16 * 4)
            pool.wait_ge(m_act.sem, m_act.at(H - 1, "mixhi"))
            pool.wait_ge(m_dve.sem, m_dve.at(H - 1, "mixlo"))
            pool.dma_start(x2[:, :, :], x_spill).then_inc(x_back, 16)
            pool.wait_ge(n_dve.sem, n_dve.at(0, f"x{KT - 1}"))
            pool.memset(acc_s[:, :, :], 0.0).then_inc(acc_zero, 1)

        def to_unit(split, taken):
            at = [-1]

            def go(slot):
                while at[0] < min(slot // PARTS, 4):
                    at[0] += 1
                    if at[0] > 0:
                        taken(at[0] - 1)
                    if at[0] < 4:
                        split(at[0] + 1)
            return go

        @block.scalar
        def _(act):
            act.sem_inc(hi_done, 2)
            act.sem_inc(evac_done, 2)
            for c in (a_act, g_act, m_act, o_act, f_act, n_act):
                act.sem_inc(c.sem, c.n)
            act.add_instruction(mybir.InstLoadActFuncSet(name=nc.get_next_instruction_name(), act_func_set_id=EXP_LN_SET,
                                                         engine=mybir.EngineType.Activation))
            act.dma_start(cst[:, :], A["table"]).then_inc(const_in, 16)
            for n, name in enumerate(("norm_pre_mix", "norm_post_mix", "norm_pre_ffn", "norm_post_ffn")):
                act.dma_start(norm_rows[KT * n:KT * n + KT], A[name][0].rearrange("(k p) -> k p", p=P)).then_inc(small_in, 16)
            act.dma_start(norm_rows[64:72], A["mlstm_norm"][0]).then_inc(small_in, 16)
            act.dma_start(norm_rows[72:80], A["gdn_norm"][0]).then_inc(small_in, 16)
            act.dma_start(tap_rows, A["gdn_conv_w"][0].rearrange("w (c p) -> (w c) p", p=P)).then_inc(small_in, 16)
            act.dma_start(n_rows, A["state_mlstm_n"][0].rearrange("b h d -> (b h) d")).then_inc(small_in, 16)
            act.dma_start(join_masks[:, :, :], A["joins"]).then_inc(joins_in, 16)
            for n, name in enumerate(("mlstm_b_i", "mlstm_b_f", "gdn_dt_bias", "gdn_A_log")):
                act.dma_start(bias8[:, n:n + 1], A[name].rearrange("l h -> h l")).then_inc(rows_in, 16)
            act.dma_start(mp[:, :], A["state_mlstm_m"][0].rearrange("b h -> h b")).then_inc(rows_in, 16)
            for c in range(3):
                act.dma_start(conv_rows[c], A["state_gdn_conv"][0].rearrange("b r n -> (b r) n")[:, c * W1:c * W1 + W1]).then_inc(rows_in, 16)

            def a(name, out, in_, fn, need=(), **kw):
                for c, x in need:
                    act.wait_ge(c.sem, c.at(0, x))
                act.wait_ge(a_act.sem, a_act.before(0, name))
                act.activation(out, in_, fn, **kw).then_inc(*a_act.step(name))
            act.wait_ge(a_dve.sem, a_dve.at(0, "ones"))
            for t, _, n in TILE:
                act.wait_ge(x_in[t], 16 * (1 if t == 1 else 2))
                a(f"ss{t}", psum[0:n, 4:8, :].rearrange("p b c -> p (b c)"), xtok[0:n, t, :], ACT.Square,
                  accum_out=ssum[0:n, t:t + 1])
            a("ln", ssum[:, 0:3], ssum[:, 0:3], ACT.Ln, scale=1.0 / D, bias=eps_c[:, 0:1])
            a("r", ssum[:, 0:3], ssum[:, 0:3], ACT.Exp, scale=-0.5)
            for k in range(KT):
                if k >= 2:
                    act.wait_ge(spill_done[k % 2], 16 * (k // 2))
                    act.wait_ge(a_dve.sem, a_dve.at(0, f"ut{k - 2}"))
                a(f"xo{k}", x_out[:, k % 2, :], psum[:, 2 + k % 4, 0:T], ACT.Copy, [(a_pe, f"x{k}")])
                a(f"uh{k}", u_hi[:, k, :], sq[:, k % 2, :], ACT.Copy, [(a_dve, f"ut{k}")])
            act.wait_ge(gates_in, 32)
            act.activation(whi[1][:, :, 0:4 * H], raw[:, 1, :, 0:4 * H], ACT.Copy).then_inc(hi_done, 1)
            split_hi(act, Unit(U_G, 0, 0))
            act.wait_ge(unit_done, 3)
            a("gates", gates[:, :], psum[0:4 * H, 1, 0:T], ACT.Copy)
            act.wait_ge(a_act.sem, a_act.at(0, "gates"))
            act.sem_inc(evac_done, 1)
            split_hi(act, Unit(U_G, 0, 1))
            act.wait_ge(rows_in, 16 * 8)
            a("ea", decay[:, :], bias8[:, 3:4], ACT.Exp)
            a("bexp", rows_g[:, T:2 * T], psum[0:H, 5, 0:T], ACT.Exp, [(a_pe, "sel")], scale=-1.0)
            a("abs", la[:, :, :], yf[:, :, :], ACT.Abs, [(a_dve, "yf1")])
            a("aexp", la[:, :, :], la[:, :, :], ACT.Exp, scale=-1.0)
            act.wait_ge(a_act.sem, a_act.at(0, "aexp"))
            a("aln", la[:, :, :], la[:, :, :], ACT.Ln, bias=eps_c[0:H, 1:2])
            a("iexp", rows_m[:, T:T + NB * DEC], rows_m[:, T:T + NB * DEC], ACT.Exp, [(a_dve, "it")])
            a("em", rows_m[:, T + NB * DEC:], m_row[:, :], ACT.Exp, [(a_dve, "msc")], scale=-1.0)
            a("eg", rows_g[:, 2 * T:], rows_g[:, 0:T], ACT.Exp, [(a_dve, "gsc")])
            a("wl", col_src[:, 1, 0:T], col_src[:, 1, 0:T], ACT.Exp, [(a_dve, "wl1")])
            a("kh", col_src[:, 5, 0:T], col_src[:, 5, 0:T], ACT.Exp, [(a_dve, "kh3")])
            act.wait_ge(a_act.sem, a_act.at(0, "kh"))

            w0 = [Unit(U_G, 0, i) for i in range(5)]
            for i in range(4):
                if i > 0:
                    split_hi(act, w0[i + 1])
                if i == 0:
                    act.wait_ge(a_pool.sem, a_pool.at(0, "z0"))
                evacuate(act, w0[i], i, "g")

            def sigmoid(s, dv, c):
                one = eps_c[:, 1:2]
                s(f"e{c}p", cs[:, c, 0:NP], y[:, c, 0:NP], ACT.Exp, [(dv, f"c{c}w3")], scale=-1.0)
                s(f"e{c}d", group_cols(cs[:, c, :]), conv_groups(y[:, c, :]), ACT.Exp, scale=-1.0)
                s(f"e{c}l", cs[:, c, 0:T], cs[:, c, 0:T], ACT.Ln, bias=one)
                s(f"e{c}s", cs[:, c, 0:T], cs[:, c, 0:T], ACT.Exp, scale=-1.0)
            s0 = lambda name, out, in_, fn, need=(), **kw: a(name, out, in_, fn, need, **kw)
            for c in range(3):
                sigmoid(s0, a_dve, c)
            s0("esq", sq[:, :, :], cs[:, 0:2, 0:T], ACT.Square, [(a_dve, "cs_d")])

            def gdn(it, kind):
                early = kind == "g"
                nxt = [Unit(U_G, it, 4 + i) for i in range(5)]

                def taken(i):
                    if i < 3:
                        act.wait_ge(g_dve.sem, g_dve.prev(it, f"c{i}w3"))
                        act.wait_ge(g_pool.sem, g_pool.at(it, "save_d"))
                    else:
                        act.wait_ge(g_dve.sem, g_dve.at(it, "gate"))
                    evacuate(act, nxt[i], i, kind)
                go = to_unit(lambda i: split_hi(act, nxt[i]), taken)

                def s(name, out, in_, fn, need=(), slot=None, **kw):
                    if slot:
                        go(SLOT_G[slot])
                    for c, x in need:
                        act.wait_ge(c.sem, c.at(it, x))
                    act.wait_ge(g_act.sem, g_act.before(it, name))
                    act.activation(out, in_, fn, **kw).then_inc(*g_act.step(name))
                go(0)
                s("ln", sq[:, :, :], psum[:, 5:7, 0:T], ACT.Ln, [(g_pe, "ss")], "ss", bias=eps_c[:, 0:1])
                s("rs", sq[:, :, :], sq[:, :, :], ACT.Exp, scale=-0.5)
                s("dec_exp", dec[:, :], dec[:, :], ACT.Exp, [(g_dve, "e2")], "bc")
                for t in range(3):
                    s(f"vb{t}", v_tok[:, t, :], B(5, t * P, t * P + P), ACT.Copy, [(g_pe, "tr")], "tr",
                      scale=cols[:, t, 4, bass.ds(it, 1)])
                act.wait_ge(g_dve.sem, g_dve.before(it, "qn"))
                s("z0", gate[:, :], stage_z[:, :], ACT.Exp, scale=-1.0)
                s("z1", gate[:, :], gate[:, :], ACT.Ln, bias=eps_c[:, 1:2])
                s("z2", gate[:, :], gate[:, :], ACT.Exp, scale=-1.0)

                def next_sigmoid(c):
                    if early:
                        sigmoid(s, g_dve, c)
                    else:
                        g_act.skip(act, it, [f"e{c}{x}" for x in "pdls"])
                for lv in range(1, LEVELS):
                    s(f"p{lv}", pb[:, 0:T], B(1), ACT.Copy, [(g_pe, f"p{lv}")], f"p{lv}")
                    if lv in (3, 6):
                        next_sigmoid(lv // 3 - 1)
                s("nkd", nkd[:, :], B(4), ACT.Copy, [(g_pe, "nkd")], "nkd")
                for t in range(3):
                    s(f"w{t}", wv[:, t, :], B(5, t * P, t * P + P), ACT.Copy, [(g_pe, f"w{t}")], f"w{t}")
                s("osq", sq[:, 0, :], B(4), ACT.Square, [(g_pe, "o")], "o")
                next_sigmoid(2)
                s("oln", fac[:, :], B(5), ACT.Ln, [(g_pe, "ms")], "ms", bias=eps_c[:, 0:1])
                s("ors", fac[:, :], fac[:, :], ACT.Exp, scale=-0.5)
                if early:
                    s("esq", sq[:, :, :], cs[:, 0:2, 0:T], ACT.Square, [(g_dve, "cs_d")])
                else:
                    g_act.skip(act, it, ["esq"])
                go(4 * PARTS)
                s("mixhi", mix_hi[:, bass.ds(it + H, 1), :].rearrange("p o t -> p (o t)"), mixf[:, :], ACT.Copy, [(g_dve, "omix")])
            with act.Fori(0, H - 1) as it:
                gdn(it, "g")
            gdn(H - 1, "m")

            def mlstm(it, last):
                own = Unit(U_M, it, 3)
                nxt = [Unit(U_M, it, 4 + i) for i in range(5)]

                def taken(i):
                    act.wait_ge(m_act.sem, m_act.at(it, "oe"))
                    evacuate(act, nxt[i], i, "m")
                go = (lambda slot: None) if last else to_unit(lambda i: split_hi(act, nxt[i]), taken)

                def s(name, out, in_, fn, need=(), slot=None, **kw):
                    if slot:
                        go(SLOT_M[slot])
                    for c, x in need:
                        act.wait_ge(c.sem, c.at(it, x))
                    act.wait_ge(m_act.sem, m_act.before(it, name))
                    act.activation(out, in_, fn, **kw).then_inc(*m_act.step(name))
                go(0)
                act.wait_ge(evac_done, own.u)
                act.wait_ge(m_dve.sem, m_dve.before(it, "o1"))
                act.wait_ge(m_pe.sem, m_pe.before(it, "bc"))
                s("q", qn[:, :], stage[:, 0, 0:T], ACT.Copy, scale=QS)
                s("k", kn[:, 0:T], stage[:, 1, 0:T], ACT.Copy)
                s("vp", vpad[:, 0:T], stage[:, 2, 0:T], ACT.Copy)
                s("oe", gate[:, :], stage_z[:, :], ACT.Exp, scale=-1.0)
                act.wait_ge(m_pool.sem, m_pool.before(it, "sel"))
                s("v", v_tok[:, :, :].rearrange("p t e -> p (t e)"), B(4, 0, TP), ACT.Copy, [(m_pe, "tr")], "tr")
                s("exp", sc_e[:, :], sc_e[:, :], ACT.Exp, [(m_dve, "e2")], "bc")
                s("absd", fac[:, :], B(2), ACT.Abs, [(m_pe, "den")], "den")
                s("hsq", sq[:, 0, :], hm[:, :], ACT.Square, [(m_dve, "h")])
                s("ln", fac[:, :], B(3), ACT.Ln, [(m_pe, "ms")], "ms", bias=eps_c[:, 0:1])
                s("rs", fac[:, :], fac[:, :], ACT.Exp, scale=-0.5)
                go(4 * PARTS)
                s("mixhi", mix_hi[:, bass.ds(it, 1), :].rearrange("p o t -> p (o t)"), mixf[:, :], ACT.Copy, [(m_dve, "mixf")])
            with act.Fori(0, H - 1) as it:
                mlstm(it, False)
            mlstm(H - 1, True)

            act.wait_ge(st_stored, 64 * H + 16)
            act.wait_ge(rows_out, 16 * 4)
            act.wait_ge(m_dve.sem, m_dve.at(H - 1, "mixlo"))
            with act.Fori(0, KT // 4) as it:
                for i in range(4):
                    split_hi(act, Unit(U_O, it, i + 1))
                    w, m = Unit(U_O, it, i), 4 * it + i
                    act.wait_ge(unit_done, w.u)
                    act.wait_ge(o_pe.sem, o_pe.before(m, "ms"))
                    act.wait_ge(o_act.sem, o_act.before(m, "copy"))
                    act.activation(acc_s[:, bass.ds(m, 1), :].rearrange("p o t -> p (o t)"), psum[:, w.slot, 0:T],
                                   ACT.Copy).then_inc(*o_act.step("copy"))
                    act.wait_ge(o_act.sem, o_act.at(m, "copy"))
                    act.activation(fsq[:, 0, :], psum[:, w.slot, 0:T], ACT.Square).then_inc(*o_act.step("sq"))
                    act.wait_ge(o_act.sem, o_act.at(m, "sq"))
                    act.sem_inc(evac_done, 1)

            def n(name, out, in_, fn, need=(), **kw):
                for c, x in need:
                    act.wait_ge(c.sem, c.at(0, x))
                act.wait_ge(n_act.sem, n_act.before(0, name))
                act.activation(out, in_, fn, **kw).then_inc(*n_act.step(name))
            act.wait_ge(o_pe.sem, o_pe.at(KT - 1, "ms"))
            n("ln", frb[:, :], psum[:, 2, 0:T], ACT.Ln, scale=1.0 / KT, bias=eps_c[:, 0:1])
            n("r", frb[:, :], frb[:, :], ACT.Exp, scale=-0.5)
            for k in range(KT):
                n(f"sq{k}", fs16[:, k, :], x2[:, k, :], ACT.Square, [(n_dve, f"x{k}")])
            n("ln2", frb[:, :], psum[:, 3, 0:T], ACT.Ln, [(n_pe, "ms2")], scale=1.0 / KT, bias=eps_c[:, 0:1])
            n("r2", frb[:, :], frb[:, :], ACT.Exp, scale=-0.5)
            for k in range(KT):
                n(f"uh{k}", u_hi[:, k, :], fsq[:, k % 2, :], ACT.Copy, [(n_dve, f"ut{k}")])

            def gate_up(group, parity, base, it, i0, per=24):
                for j in range(4):
                    q = 4 * group + j
                    g, u = (Unit(base, it, i0 + 2 * j + x, per) for x in range(2))
                    split_hi(act, Unit(base, it, i0 + 2 * j + 1, per))
                    act.wait_ge(unit_done, g.u)
                    act.wait_ge(f_dve.sem, f_dve.before(q, "add"))
                    act.wait_ge(f_act.sem, f_act.before(q, "e"))
                    act.activation(fe[:, :], psum[:, 2 * (j % 2), 0:T], ACT.Exp, scale=-1.0).then_inc(*f_act.step("e"))
                    split_hi(act, Unit(base, it, i0 + 2 * j + 2, per))
                    act.wait_ge(f_dve.sem, f_dve.at(q, "h"))
                    act.wait_ge(f_act.sem, f_act.before(q, "hi"))
                    act.activation(h_hi[:, parity, j, :], fh[:, :], ACT.Copy).then_inc(*f_act.step("hi"))

            def down(base, it, i0, per=24, last=False):
                for n_ in range(3 if last else 4):
                    split_hi(act, Unit(base, it, i0 + n_ + 1, per))
            gate_up(0, 0, U_F, 0, 0)
            with act.Fori(0, FG // 2) as it:
                for half in range(2):
                    gate_up(2 * it + 1 + half, 1 - half, U_F + 8, it, 12 * half)
                    down(U_F + 8, it, 12 * half + 8)
            down(U_END - 4, 0, 0, last=True)
            act.wait_ge(added.sem, added.at(FG - 1, "3"))
            for k in range(KT):
                n(f"fq{k}", fs16[:, k, :], acc_s[:, k, :], ACT.Square)
            n("ln3", frb[:, :], psum[:, 2, 0:T], ACT.Ln, [(n_pe, "ffn")], scale=1.0 / KT, bias=eps_c[:, 0:1])
            n("r3", frb[:, :], frb[:, :], ACT.Exp, scale=-0.5)
            for k in range(KT):
                b = k // 4 % 2
                if k % 4 == 0 and k >= 8:
                    act.wait_ge(y_out[b], 64 * (k // 8))
                act.wait_ge(n_pe.sem, n_pe.at(0, f"y{k}"))
                act.activation(y_tok[:, b, 0:2, k % 4, :], psum[:, 3 + k % 4, 0:2 * P].rearrange("p (t d) -> p t d", t=2), ACT.Copy)
                n(f"yc{k}", y_tok[0:T2, b, 2, k % 4, :], psum[0:T2, 3 + k % 4, 2 * P:TP], ACT.Copy)

        @block.tensor
        def _(pe):
            pe.sem_inc(unit_done, 2)
            for c in (a_pe, g_pe, m_pe, o_pe, n_pe, tail):
                pe.sem_inc(c.sem, c.n)

            def wait(it, *need):
                for c, x in need:
                    pe.wait_ge(c.sem, c.at(it, x))

            def mm(out, a, b, start=True, stop=True):
                return pe.matmul(out, a, b, start=start, stop=stop, skip_group_check=True)

            pe.wait_ge(const_in, 16)
            pe.wait_ge(small_in, 16 * 8)
            pe.transpose(psum[:, 0, 0:80], norm_rows, ident[0:80, 0:80])
            pe.transpose(psum[:, 0, 80:176], tap_rows, ident[0:96, 0:96])
            pe.transpose(psum[:, 0, 176:240], n_rows, ident[0:64, 0:64]).then_inc(*a_pe.step("norms"))
            wait(0, (a_dve, "dg2"))
            for t, s0, n in TILE:
                ins = mm(psum[:, 1, s0:s0 + n], ones, v_tok[:, t, 0:n], start=(t == 0), stop=(t == 2))
            ins.then_inc(*a_pe.step("rb"))
            for k in range(KT):
                if k >= 4:
                    wait(0, (a_act, f"xo{k - 4}"))
                for t, s0, n in TILE:
                    ins = pe.transpose(psum[:, 2 + k % 4, s0:s0 + n], xtok[0:n, t, k * P:k * P + P], ident[0:n, 0:n])
                ins.then_inc(*a_pe.step(f"x{k}"))
            pe.wait_ge(lo_done, 3)
            wait(0, (a_dve, "rb"))
            for k in range(KT):
                if k % 4 == 0:
                    wait(0, (a_dve, f"ul{k + 3}"))
                ins = products(pe, psum[0:4 * H, 1, 0:T], [(whi[1][:, k, 0:4 * H], wlo[1][:, k, 0:4 * H],
                                                            u_hi[:, k, :], u_lo[:, k, :])], k == 0, k == KT - 1)
            ins.then_inc(unit_done, 1)
            for part in range(PARTS):
                if part == 0:
                    wait(0, (a_dve, "n_in"))
                unit_part(pe, Unit(U_G, 0, 0), part, u_hi, u_lo, lo_done)
            wait(0, (a_act, "gates"))
            for q in range(4):
                ins = mm(psum[0:H, 2 + q, 0:T], ident[0:4 * H, q * H:q * H + H], gates[:, :])
            ins.then_inc(*a_pe.step("sel"))
            for part in range(PARTS):
                unit_part(pe, Unit(U_G, 0, 1), part, u_hi, u_lo, lo_done)
            wait(0, (a_dve, "bc"), (a_act, "kh"), (a_act, "wl"))
            for t in range(3):
                for q in range(6):
                    c0 = (t * 6 + q) * H
                    ins = mm(psum[:, 2, c0:c0 + H], col_src[:, q, t * P:t * P + P], ident[0:H, 0:H],
                             start=(t == 0 and q == 0), stop=(t == 2 and q == 5))
            ins.then_inc(*a_pe.step("cols"))
            pe.wait_ge(rows_in, 16 * 8)
            for ct in range(3 * H):
                ins = pe.transpose(psum[:, 6 + ct // 12, (ct % 12) * 24:(ct % 12) * 24 + 24],
                                   conv_rows[ct // H][:, (ct % H) * P:(ct % H) * P + P], ident[0:24, 0:24])
            ins.then_inc(*a_pe.step("conv"))
            for i in range(2, 4):
                for part in range(PARTS):
                    unit_part(pe, Unit(U_G, 0, i), part, u_hi, u_lo, lo_done)

            def interleave(steps, slots, unit):
                todo = [(slots[name], name, fn) for name, fn in steps]
                for slot in range(4 * PARTS + 1):
                    while todo and (todo[0][0] <= slot or slot == 4 * PARTS):
                        todo.pop(0)[2]()
                    if slot < 4 * PARTS and unit is not None:
                        unit_part(pe, unit(slot // PARTS), slot % PARTS, u_hi, u_lo)

            def gdn(it):
                def bc():
                    wait(it, (g_pool, "sel"))
                    pe.wait_ge(g_dve.sem, g_dve.before(it, "qn"))
                    for q, (bank, row) in enumerate(((0, 0), (1, 1), (2, 2))):
                        ins = mm(B(bank), sel[:, :], rows_g[:, row * T:row * T + T])
                    ins.then_inc(*g_pe.step("bc"))

                def ss():
                    pe.wait_ge(g_act.sem, g_act.prev(it, "esq"))
                    mm(B(3), ones, sq[:, 0, :])
                    mm(B(4), ones, sq[:, 1, :]).then_inc(*g_pe.step("ss"))

                def kk():
                    wait(it, (g_act, "ln"), (g_dve, "kb"))
                    for t, s0, n in TILE:
                        mm(B(3, s0, s0 + n), kn[:, t * P:t * P + P], kb[:, s0:s0 + n], t == 0, t == 2)
                    for t, s0, n in TILE:
                        ins = mm(B(4, s0, s0 + n), kn[:, t * P:t * P + P], qn[:, s0:s0 + n], t == 0, t == 2)
                    ins.then_inc(*g_pe.step("kk"))

                def tr():
                    wait(it, (g_dve, "e2"))
                    for t in range(3):
                        pe.transpose(B(5, t * P, t * P + P), cs[:, 2, t * P:t * P + P], ident)
                    for t in range(3):
                        ins = pe.transpose(B(0, t * P, t * P + P), kn[:, t * P:t * P + P], ident)
                    ins.then_inc(*g_pe.step("tr"))

                def l0():
                    wait(it, (g_dve, "nat"), (g_pool, "ui"))
                    for t, s0, n in TILE:
                        ins = mm(B(2, s0, s0 + n), nat[:, t * P:t * P + P], ident[:, 0:n], t == 0, t == 2)
                    ins.then_inc(*g_pe.step("l0"))

                def p(lv):
                    def go():
                        wait(it, (g_dve, f"t{lv - 1}"), (g_dve, "kb"))
                        for t, s0, n in TILE:
                            ins = mm(B(1, s0, s0 + n), nat[:, t * P:t * P + P], tinv[:, t, 0:n], t == 0, t == 2)
                        ins.then_inc(*g_pe.step(f"p{lv}"))
                    return go

                def q(lv):
                    def go():
                        wait(it, (g_act, f"p{lv}"), (g_dve, f"u{lv - 1}"))
                        for t, s0, n in TILE:
                            mm(B(2, s0, s0 + n), uinv[:, t, :], pb[:, s0:s0 + n], t == 0, t == 2)
                        for t, s0, n in TILE:
                            ins = mm(B(3, s0, s0 + n), pb[:, t * P:t * P + P], uinv[:, t, 0:n], t == 0, t == 2)
                        ins.then_inc(*g_pe.step(f"q{lv}"))
                    return go

                def nkd_():
                    wait(it, (g_dve, f"u{LEVELS - 1}"), (g_dve, "qkd"), (g_dve, "kb2"))
                    for t, s0, n in TILE:
                        ins = mm(B(4, s0, s0 + n), k_tok[:, t, :], uinv[:, t, 0:n], t == 0, t == 2)
                    ins.then_inc(*g_pe.step("nkd"))

                def w0():
                    wait(it, (g_act, "vb2"))
                    mm(B(5, 0, P), uinv[:, 0, :], v_tok[:, 0, :]).then_inc(*g_pe.step("w0"))

                def s1():
                    wait(it, (g_act, "w0"), (g_dve, "kh2"))
                    mm(B(0, 0, P), kh_tok[:, 0, :], wv[:, 0, :]).then_inc(*g_pe.step("s1"))

                def w1():
                    wait(it, (g_dve, "s1"), (g_act, "nkd"))
                    mm(B(5, P, 2 * P), uinv[:, 1, :], v_tok[:, 1, :], True, False)
                    mm(B(5, P, 2 * P), nkd[:, P:2 * P], s_chunk[:, 0, :], False, True).then_inc(*g_pe.step("w1"))

                def s2():
                    wait(it, (g_act, "w1"))
                    mm(B(0, P, 2 * P), kh_tok[:, 1, :], wv[:, 1, :]).then_inc(*g_pe.step("s2"))

                def w2():
                    wait(it, (g_dve, "s2"), (g_dve, "nkdm"))
                    pe.wait_ge(st_loaded, 16 * (it + 1))
                    mm(B(5, 2 * P, 3 * P), uinv[:, 2, :], v_tok[:, 2, :], True, False)
                    out = psum[0:T2, 7, 2 * P:3 * P]
                    for b in range(NB):
                        mm(out, nkdm[:, b, :], st_in[:, b, :], False, False)
                    mm(out, nkdm[:, NB, :], s_chunk[:, 1, :], False, True).then_inc(*g_pe.step("w2"))

                def o():
                    wait(it, (g_act, "w2"), (g_dve, "qeg"))
                    for t, s0, n in TILE:
                        mm(B(4, s0, s0 + n), wv[:, t, :], dec[:, s0:s0 + n], t == 0, False)
                    mm(B(4, P, 2 * P), s_chunk[:, 0, :], qeg[:, P:2 * P], False, False)
                    mm(B(4, 2 * P, NP), s_chunk[:, 1, :], qeg[:, 2 * P:NP], False, False)
                    for b in range(NB):
                        c0 = NP + b * DEC
                        ins = mm(B(4, c0, c0 + DEC), st_in[:, b, :], qeg[:, c0:c0 + DEC], False, b == NB - 1)
                    ins.then_inc(*g_pe.step("o"))

                def st():
                    wait(it, (g_pool, "wm"), (g_dve, f"t{LEVELS - 1}"))
                    for bank, g0, gn in ((1, 0, 4), (2, 4, 4), (3, 8, 1)):
                        ins = mm(B(bank, 0, gn * P), kh_tok[0:T2, 2, :], vm[:, g0:g0 + gn, :])
                    ins.then_inc(*g_pe.step("st"))

                def ms():
                    wait(it, (g_act, "osq"))
                    mm(B(5), mean, sq[:, 0, :]).then_inc(*g_pe.step("ms"))
                return [("bc", bc), ("ss", ss), ("kk", kk), ("tr", tr), ("l0", l0)] \
                    + [x for lv in range(1, LEVELS) for x in ((f"p{lv}", p(lv)), (f"q{lv}", q(lv)))] \
                    + [("nkd", nkd_), ("w0", w0), ("s1", s1), ("w1", w1), ("s2", s2), ("w2", w2), ("o", o), ("st", st), ("ms", ms)]
            wait(0, (a_act, "esq"))
            with pe.Fori(0, H - 1) as it:
                interleave(gdn(it), SLOT_G, lambda i: Unit(U_G, it, 4 + i))
            interleave(gdn(H - 1), SLOT_G, lambda i: Unit(U_G, H - 1, 4 + i))

            def mlstm(it):
                def tr():
                    wait(it, (m_act, "vp"))
                    pe.wait_ge(pads_ready, H + 1)
                    for t in range(3):
                        pe.transpose(B(3, t * P, t * P + P), kn[:, t * P:t * P + P], ident)
                    for t in range(3):
                        ins = pe.transpose(B(4, t * P, t * P + P), vpad[:, t * P:t * P + P], ident)
                    ins.then_inc(*m_pe.step("tr"))

                def bc():
                    wait(it, (m_pool, "sel"))
                    pe.wait_ge(m_dve.sem, m_dve.before(it, "o1"))
                    mm(B(0, 0, T + NB * DEC), sel[:, :], rows_m[:, 0:T + NB * DEC])
                    mm(B(1), sel[:, :], rows_m[:, T + NB * DEC:]).then_inc(*m_pe.step("bc"))

                def sc():
                    wait(it, (m_act, "k"))
                    for t, a, b, c0 in ((0, 0, NP, 0), (1, P, NP, NP), (2, 2 * P, T, NP + NP - P)):
                        ins = mm(B(2, c0, c0 + b - a), kn[:, t * P:t * P + P], qn[:, a:b], t == 0, t == 2)
                    ins.then_inc(*m_pe.step("sc"))

                def over_keys(bank, lhs):
                    for t, a, b, c0 in ((0, 0, NP, 0), (1, P, NP, NP), (2, 2 * P, T, NP + NP - P)):
                        mm(B(bank, a, b), lhs(t), sc_p[:, c0:c0 + b - a], t == 0, False)

                def num():
                    wait(it, (m_dve, "pm"), (m_act, "v"), (m_dve, "qi"))
                    pe.wait_ge(st_loaded, 16 * (it + H + 1))
                    over_keys(5, lambda t: v_tok[:, t, :])
                    for b in range(NB):
                        c0 = NP + b * DEC
                        ins = mm(B(5, c0, c0 + DEC), st_in[:, b, :], qi[:, b * DEC:b * DEC + DEC], False, b == NB - 1)
                    ins.then_inc(*m_pe.step("num"))

                def den():
                    wait(it, (m_dve, "nq"))
                    over_keys(2, lambda t: ones)
                    mm(B(2, NP, T), ones, nq[:, :], False, True).then_inc(*m_pe.step("den"))

                def st():
                    wait(it, (m_dve, "kw2"), (m_pool, "vm"), (m_dve, "dmax"))
                    mm(B(4, 0, 4 * P), k_tok[0:T2, 2, :], vm[:, 0:4, :])
                    mm(B(0, 0, 4 * P), k_tok[0:T2, 2, :], vm[:, 4:8, :])
                    mm(B(1, 0, P), k_tok[0:T2, 2, :], vm[:, 8, :], True, False)
                    mm(B(1, P, P + NG), k_tok[0:T2, 2, :], C("gmask", T2), False, False)
                    for t in range(2):
                        mm(B(1, 0, P), k_tok[:, t, :], v_tok[:, t, :], False, False)
                        ins = mm(B(1, P + NB, P + NG), k_tok[:, t, :], ones[:, 0:1], False, t == 1)
                    ins.then_inc(*m_pe.step("st"))

                def ms():
                    wait(it, (m_act, "hsq"))
                    mm(B(3), mean, sq[:, 0, :]).then_inc(*m_pe.step("ms"))
                return [("bc", bc), ("tr", tr), ("sc", sc), ("num", num), ("den", den), ("st", st), ("ms", ms)]
            with pe.Fori(0, H - 1) as it:
                interleave(mlstm(it), SLOT_M, lambda i: Unit(U_M, it, 4 + i))
            interleave(mlstm(H - 1), SLOT_M, None)

            pe.wait_ge(m_dve.sem, m_dve.at(H - 1, "mixlo"))
            for n in range(6):
                if n >= 2:
                    wait(0, (tail_v, f"c{n - 2}"))
                for x in range(4):
                    ct = 4 * n + x
                    ins = pe.transpose(psum[0:NG * 3, 6 + n % 2, x * P:x * P + P], conv_out[:, ct // H, ct % H, :], ident)
                ins.then_inc(*tail.step(f"c{n}"))
            wait(0, (tail_v, "c5"))
            pe.wait_ge(m_dve.sem, m_dve.at(H - 1, "np"))
            pe.transpose(psum[0:NG * H, 6, 0:P], n_out[:, :, :].rearrange("p g h -> p (g h)"), ident).then_inc(*tail.step("n"))

            pe.wait_ge(m_dve.sem, m_dve.at(H - 1, "mixlo"))

            def sum_squares(m):
                wait(m, (o_act, "sq"))
                first = isinstance(m, int) and m == 0
                mm(psum[:, 2, 0:T], mean, fsq[:, 0, :], first, isinstance(m, int) and m == KT - 1).then_inc(*o_pe.step("ms"))

            def o_unit(it, i, sums):
                w = Unit(U_O, it, i)
                pe.wait_ge(lo_pool if isinstance(it, int) and it + i == 0 else lo_done, w.u)
                pe.wait_ge(evac_done, w.u - 2)
                products(pe, psum[:, w.slot, 0:T], tiles(w, range(8), mix_hi, mix_lo), True, False)
                if sums:
                    sum_squares(4 * it + i - 1)
                products(pe, psum[:, w.slot, 0:T], tiles(w, range(8, KT), mix_hi, mix_lo), False, True).then_inc(unit_done, 1)
            for i in range(4):
                o_unit(0, i, i > 0)
            with pe.Fori(1, KT // 4) as it:
                for i in range(4):
                    o_unit(it, i, True)
            sum_squares(KT - 1)

            for k in range(KT):
                wait(0, (n_act, f"sq{k}"))
                ins = mm(psum[:, 3, 0:T], mean, fs16[:, k, :], k == 0, k == KT - 1)
            ins.then_inc(*n_pe.step("ms2"))

            def gate_up(group, base, it, i0, per=24, first=False):
                for j in range(4):
                    q = 4 * group + j
                    for x in range(2):
                        w = Unit(base, it, i0 + 2 * j + x, per)
                        pe.wait_ge(lo_done, w.u)
                        if not isinstance(q, int) or q >= 2:
                            pe.wait_ge(f_dve.sem, f_dve.at(q - 2, "s" if x == 0 else "h"))
                        out = psum[:, 2 * (j % 2) + x, 0:T]
                        for k0 in range(0, KT, 4):
                            if first and j == 0 and x == 0:
                                wait(0, (n_dve, f"ut{k0 + 3}"), (n_act, f"uh{k0 + 3}"), (n_dve, f"ul{k0 + 3}"))
                            ins = products(pe, out, tiles(w, range(k0, k0 + 4), u_hi, u_lo), k0 == 0, k0 == KT - 4)
                        ins.then_inc(unit_done, 1)

            def down(group, parity, base, it, i0, per=24):
                pe.wait_ge(f_dve.sem, f_dve.at(4 * group + 3, "lo"))
                for n in range(4):
                    w = Unit(base, it, i0 + n, per)
                    pe.wait_ge(lo_done, w.u)
                    pe.wait_ge(added.sem, added.before(group, str(n)))
                    for m in range(4):
                        ins = products(pe, psum[:, 4 + m, 0:T],
                                       [(whi[w.slot][:, 4 * k + m, :], wlo[w.slot][:, 4 * k + m, :],
                                         h_hi[:, parity, k, :], h_lo[:, parity, k, :]) for k in range(4)], True, True)
                    ins.then_inc(unit_done, 1)
            pe.wait_ge(evac_done, U_F - 1)
            gate_up(0, U_F, 0, 0, first=True)
            with pe.Fori(0, FG // 2) as it:
                for half in range(2):
                    gate_up(2 * it + 1 + half, U_F + 8, it, 12 * half)
                    down(2 * it + half, half, U_F + 8, it, 12 * half + 8)
            down(FG - 1, 0, U_END - 4, 0, 0)
            for k in range(KT):
                wait(0, (n_act, f"fq{k}"))
                ins = mm(psum[:, 2, 0:T], mean, fs16[:, k, :], k == 0, k == KT - 1)
            ins.then_inc(*n_pe.step("ffn"))
            for k in range(KT):
                if k >= 4:
                    wait(0, (n_act, f"yc{k - 4}"))
                wait(0, (n_dve, f"fx{k}"))
                for t, s0, n in TILE:
                    ins = pe.transpose(psum[0:n, 3 + k % 4, t * P:t * P + P], acc_s[:, k, s0:s0 + n], ident)
                ins.then_inc(*n_pe.step(f"y{k}"))

        @block.vector
        def _(dve):
            dve.sem_inc(lo_done, 2)
            for c in (a_dve, g_dve, m_dve, f_dve, added, n_dve, tail_v):
                dve.sem_inc(c.sem, c.n)

            def runner(own, it):
                def s(name, op, *args, need=(), **kw):
                    for c, x in need:
                        dve.wait_ge(c.sem, c.at(it, x))
                    dve.wait_ge(own.sem, own.before(it, name))
                    if op == dve.copy_predicated:
                        dve.sem_inc(join_turn, 1)
                    op(*args, **kw).then_inc(*own.step(name))
                return s
            copy, tt, ts, stt = dve.tensor_copy, dve.tensor_tensor, dve.tensor_scalar, dve.scalar_tensor_tensor

            a = runner(a_dve, 0)
            dve.memset(ssum[:, :], 1.0)
            for n, v in enumerate((EPS, 1.0, float(np.log(QS)))):
                dve.memset(eps_c[:, n:n + 1], v)
            a("ones", dve.memset, m8[:, :], 0.0)
            a("norms", copy, norms[:, :], psum[:, 0, 0:80], need=[(a_pe, "norms")])
            a("convw", copy, convw[:, :], psum[:, 0, 80:176])
            a("n_in", copy, n_in[:, :], psum[:, 0, 176:240])
            for t in range(3):
                a(f"dg{t}", ts, v_tok[:, t, :], ident, ssum[:, t:t + 1], None, ALU.mult, need=[(a_act, "r")])
            a("rb", copy, fac[:, :], psum[:, 1, 0:T], need=[(a_pe, "rb")])
            for k in range(KT):
                if k >= 2:
                    dve.wait_ge(a_act.sem, a_act.at(0, f"uh{k - 2}"))
                a(f"ut{k}", stt, sq[:, k % 2, :], x_out[:, k % 2, :], norms[:, k:k + 1], fac[:, :], ALU.mult, ALU.mult,
                  need=[(a_act, f"xo{k}")])
                a(f"ul{k}", tt, u_lo[:, k, :], sq[:, k % 2, :], u_hi[:, k, :].bitcast(F32), ALU.subtract,
                  need=[(a_act, f"uh{k}")])
            dve.wait_ge(hi_done, 3)
            dve.tensor_tensor(wlo[1][:, :, 0:4 * H], raw[:, 1, :, 0:4 * H], whi[1][:, :, 0:4 * H].bitcast(F32),
                              ALU.subtract).then_inc(lo_done, 1)
            split_lo(dve, Unit(U_G, 0, 0))
            dve.wait_ge(rows_in, 16 * 8)
            bias = lambda n: bias8[:, n:n + 1]
            a("li", ts, li[:, :], psum[0:H, 2, 0:T], bias(0), None, ALU.add, need=[(a_pe, "sel")])
            a("yf0", ts, yf[:, 0, :], psum[0:H, 3, 0:T], bias(1), None, ALU.add)
            a("yf1", ts, yf[:, 1, :], psum[0:H, 4, 0:T], bias(2), None, ALU.add)
            split_lo(dve, Unit(U_G, 0, 1))
            G_, BT, EG = (rows_g[:, n * T:n * T + T] for n in range(3))
            R_, IN = rows_m[:, 0:T], rows_m[:, T:T + NB * DEC]
            a("b1", ts, BT, BT, 1.0, None, ALU.add, need=[(a_act, "bexp")])
            a("b2", dve.reciprocal, BT, BT)
            a("lf", stt, yf[:, 0, :], yf[:, 0, :], 0.0, la[:, 0, :], ALU.min, ALU.subtract, need=[(a_act, "aln")])
            a("sp", stt, yf[:, 1, :], yf[:, 1, :], 0.0, la[:, 1, :], ALU.max, ALU.add)
            a("lg", ts, yf[:, 1, :], yf[:, 1, :], decay[:, 0:1], -1.0, ALU.mult, ALU.mult)
            dve.wait_ge(st_stored, 16)
            a("bsc", dve.tensor_tensor_scan, b_row[:, :], scan_m[:, 0, :], yf[:, 0, :], 0.0, ALU.mult, ALU.add)
            a("gsc", dve.tensor_tensor_scan, G_, scan_m[:, 1, :], yf[:, 1, :], 0.0, ALU.mult, ALU.add)
            dve.wait_ge(a_pool.sem, a_pool.at(0, "z2"))
            a("c", tt, col_src[:, 0, 0:T], li[:, :], b_row[:, :], ALU.subtract)
            lf0, li0 = group_cols(yf[:, 0, :])[:, :, 0], group_cols(li)[:, :, 0]
            a("mx0", tt, li[:, 0:1], li[:, 0:1], yf[:, 0, 0:1], ALU.max)
            a("t8", tt, m8[:, :], lf0, mp[:, :], ALU.add)
            a("mx1", tt, li0, li0, m8[:, :], ALU.max)
            a("ng0", dve.memset, yf[:, 0, 0:1], NEG)
            a("ng1", dve.memset, lf0, NEG)
            a("msc", dve.tensor_tensor_scan, m_row[:, :], yf[:, 0, :], li[:, :], 0.0, ALU.add, ALU.max)
            a("r", tt, R_, b_row[:, :], m_row[:, :], ALU.subtract)
            spread_g = lambda x: x.unsqueeze(2).to_broadcast([H, NB, DEC])
            a("it", tt, group_cols(IN, 0), group_cols(R_), spread_g(mp[:, :]), ALU.add)
            end = lambda x: group_cols(x)[:, :, DEC - 1]
            a("wl0", ts, col_src[:, 1, 0:NP], col_src[:, 0, 0:NP], R_[:, NP - 1:NP], None, ALU.add)
            a("wl1", tt, group_cols(col_src[:, 1, :]), group_cols(col_src[:, 0, :]), spread_g(end(R_)), ALU.add)
            a("ngg", ts, col_src[:, 2, 0:T], G_, -1.0, None, ALU.mult)
            for n, (x, z) in enumerate(((0, P), (P, 2 * P), (2 * P, NP))):
                a(f"kh{n}", ts, col_src[:, 5, x:z], G_[:, x:z], -1.0, G_[:, z - 1:z], ALU.mult, ALU.add)
            a("kh3", tt, group_cols(col_src[:, 5, :]), spread_g(end(G_)), group_cols(G_), ALU.subtract)
            a("nb", stt, col_src[:, 3, 0:T], BT, -1.0, EG, ALU.mult, ALU.mult, need=[(a_act, "eg")])
            a("bc", copy, col_src[:, 4, 0:T], BT)
            split_lo(dve, Unit(U_G, 0, 2))
            a("cols", copy, cols[:, :, :, :].rearrange("p t q h -> p (t q h)"), psum[:, 2, 0:144], need=[(a_pe, "cols")])
            for n in range(2):
                flat = conv_in[:, :, :, :].rearrange("p c h r -> p (c h r)")
                a(f"ci{n}", copy, flat[:, 288 * n:288 * n + 288], psum[:, 6 + n, 0:288], need=[(a_pe, "conv")])
            split_lo(dve, Unit(U_G, 0, 3))

            flat3 = lambda x: x[:, :, :].rearrange("p t n -> p (t n)")

            def convolve(s, c, head, taps):
                for i in taps:
                    w = convw[:, bass.ds(head + (i * 3 * H + c * H), 1)]
                    if i == 0:
                        s(f"c{c}w0", ts, y[:, c, :], stage[:, c, 0:YW], w, None, ALU.mult)
                    else:
                        s(f"c{c}w{i}", stt, y[:, c, :], stage[:, c, i:i + YW], w, y[:, c, :], ALU.mult, ALU.add)

            def silu(s, ac):
                s("cs_p", tt, cs[:, :, 0:NP], cs[:, :, 0:NP], y[:, :, 0:NP], ALU.mult, need=[(ac, "e2s")])
                for c in range(3):
                    args = group_cols(cs[:, c, :]), group_cols(cs[:, c, :]), conv_groups(y[:, c, :]), ALU.mult
                    if c < 2:
                        dve.tensor_tensor(*args)
                    else:
                        s("cs_d", tt, *args)
            dve.wait_ge(pads_ready, 1)
            for c in range(3):
                dve.wait_ge(evac_done, Unit(U_G, 0, c).u)
                convolve(a, c, 0, range(TAPS))
            dve.wait_ge(a_pool.sem, a_pool.at(0, "joins"))
            silu(a, a_act)

            def gdn(it, last):
                nxt = [Unit(U_G, it, 4 + i) for i in range(3)]
                s = runner(g_dve, it)

                def next_conv(c, taps):
                    if last:
                        g_dve.skip(dve, it, [f"c{c}w{i}" for i in taps])
                        return
                    if taps[0] == 0:
                        dve.wait_ge(evac_done, nxt[c].u)
                        dve.wait_ge(pads_ready, it + 2)
                    convolve(s, c, it + 1, taps)
                s("qn", stt, qn[:, :], cs[:, 0, 0:T], QS, sq[:, 0, :], ALU.mult, ALU.mult, need=[(g_act, "rs")])
                s("kn", tt, kn[:, 0:T], cs[:, 1, 0:T], sq[:, 1, :], ALU.mult)
                s("kb", tt, kb[:, :], kn[:, 0:T], B(1), ALU.mult, need=[(g_pe, "bc")])
                s("qeg", tt, qeg[:, :], qn[:, :], B(2), ALU.mult)
                s("d1", copy, dcs[:, 0:1], B(2, 2 * P - 1, 2 * P))
                s("d2", copy, dcs[:, 1:2], B(2, NP - 1, NP))
                s("d3", copy, dcs[:, 2:2 + NB], group_cols(B(2))[:, :, DEC - 1])
                for t, s0, n in TILE:
                    s(f"e{t}", stt, dec[:, s0:s0 + n], B(0, s0, s0 + n), cols[:, t, 2, bass.ds(it, 1)],
                      C("cap_g")[:, s0:s0 + n], ALU.add, ALU.min)
                s("qkd", tt, dec[:, :], dec[:, :], B(4), ALU.mult, need=[(g_pe, "kk"), (g_pool, "decn")])
                s("nat", tt, nat[:, 0:T], decn[:, :], B(3), ALU.mult)
                for t in range(3):
                    s(f"kb{t}", ts, k_tok[:, t, :], B(0, t * P, t * P + P), cols[:, t, 3, bass.ds(it, 1)], None, ALU.mult,
                      need=[(g_pe, "tr")])
                for t in range(3):
                    s(f"kh{t}", ts, kh_tok[:, t, :], B(0, t * P, t * P + P), cols[:, t, 5, bass.ds(it, 1)], None, ALU.mult)
                s("gate", tt, gate[:, :], gate[:, :], stage_z[:, :], ALU.mult, need=[(g_act, "z2")])
                join = lambda n: joins[:, n, :]
                s("t0", dve.copy_predicated, flat3(tinv)[:, 0:T], join(0), B(2), need=[(g_pe, "l0"), (g_pool, "ti")])
                s("u0", dve.copy_predicated, flat3(uinv)[:, 0:T], join(LEVELS), nat[:, 0:T], need=[(g_pool, "ui")])
                for lv in range(1, LEVELS):
                    if lv in (2, 3, 5, 6):
                        next_conv(lv // 4, (0, 1) if lv in (2, 5) else (2, 3))
                    s(f"t{lv}", dve.copy_predicated, flat3(tinv)[:, 0:T], join(lv), B(2), need=[(g_pe, f"q{lv}")])
                    s(f"u{lv}", dve.copy_predicated, flat3(uinv)[:, 0:T], join(LEVELS + lv), B(3))
                s("nkdm", tt, nkdm[:, :, :], nkd[:, 2 * P:T].unsqueeze(1).to_broadcast([P, NG, T2]),
                  C("gmask_rows").rearrange("p (g t) -> p g t", g=NG), ALU.mult, need=[(g_act, "nkd")])
                s("s1", copy, s_chunk[:, 0, :], B(0, 0, P), need=[(g_pe, "s1")])
                s("s2", stt, s_chunk[:, 1, :], s_chunk[:, 0, :], dcs[:, 0:1], B(0, P, 2 * P), ALU.mult, ALU.add,
                  need=[(g_pe, "s2")])
                next_conv(2, range(TAPS))
                for n in range(2):
                    s(f"so{n}", tt, st_out[:, 4 * n:4 * n + 4, :], st_out[:, 4 * n:4 * n + 4, :],
                      B(1 + n, 0, 512).rearrange("p (g e) -> p g e", g=4), ALU.add, need=[(g_pe, "st"), (g_pool, "sdec")])
                dve.wait_ge(st_stored, 32 * it + 16)
                s("sp", stt, st_out[:, NB, :], s_chunk[:, 1, :], dcs[:, 1:2], B(3, 0, P), ALU.mult, ALU.add)
                if last:
                    g_dve.skip(dve, it, ["cs_p", "cs_d"])
                else:
                    silu(s, g_act)
                s("omul", stt, mixf[:, :], B(4), norms[:, bass.ds(72 + it, 1)], fac[:, :], ALU.mult, ALU.mult,
                  need=[(g_act, "ors")])
                s("omix", tt, mixf[:, :], mixf[:, :], gate[:, :], ALU.mult)
                s("mixlo", tt, mix_lo[:, bass.ds(it + H, 1), :].rearrange("p o t -> p (o t)"), mixf[:, :],
                  mix_hi[:, bass.ds(it + H, 1), :].rearrange("p o t -> p (o t)").bitcast(F32), ALU.subtract, need=[(g_act, "mixhi")])
            with dve.Fori(0, H - 1) as it:
                gdn(it, False)
            gdn(H - 1, True)

            def mlstm(it):
                s = runner(m_dve, it)
                s("o1", ts, gate[:, :], gate[:, :], 1.0, None, ALU.add, need=[(m_act, "oe")])
                s("gate", dve.reciprocal, gate[:, :], gate[:, :])
                col = lambda t, q: cols[:, t, q, bass.ds(it, 1)]
                for t, x, z, c0 in ((0, 0, NP, 0), (1, P, NP, NP), (2, 2 * P, T, NP + NP - P)):
                    s(f"e{t}", stt, sc_e[:, c0:c0 + z - x], B(0, x, z), col(t, 0), C("cap_m")[:, c0:c0 + z - x],
                      ALU.add, ALU.min, need=[(m_pe, "bc")])
                for t in range(3):
                    s(f"kw{t}", ts, k_tok[:, t, :], B(3, t * P, t * P + P), col(t, 1), None, ALU.mult, need=[(m_pe, "tr")])
                s("pm", tt, sc_p[:, :], sc_e[:, :], B(2, 0, 464), ALU.mult, need=[(m_act, "exp"), (m_pe, "sc")])
                s("qi", tt, qi[:, :], qn[:, NP:T], B(0, T, T + NB * DEC), ALU.mult)
                s("nq", tt, group_cols(nq, 0), group_cols(qi, 0),
                  n_in[:, :].rearrange("p (b h) -> p b h", h=H)[:, :, bass.ds(it, 1)].to_broadcast([P, NB, DEC]), ALU.mult)
                s("dcp", copy, dcs[:, 0:NB], group_cols(B(0, T, T + NB * DEC), 0)[:, :, DEC - 1])
                s("dmax", tt, fac[:, :], fac[:, :], B(1), ALU.max, need=[(m_act, "absd")])
                s("drec", dve.reciprocal, fac[:, :], fac[:, :])
                s("h", tt, hm[:, :], fac[:, :], B(5), ALU.mult)
                s("nm", tt, nm[:, :], n_in[:, :].rearrange("p (b h) -> p b h", h=H)[:, :, bass.ds(it, 1)].rearrange("p b o -> p (b o)"),
                  dcs[:, 0:NB], ALU.mult)
                n_at = lambda g0, g1: n_out[:, g0:g1, bass.ds(it, 1)].rearrange("p g o -> p (g o)")
                s("na", tt, n_at(0, NB), nm[:, :], B(1, P, P + NB), ALU.add, need=[(m_pe, "st")])
                s("np", copy, n_at(NB, NG), B(1, P + NB, P + NG))
                for n in range(2):
                    s(f"co{n}", tt, st_out[:, 4 * n:4 * n + 4, :], st_out[:, 4 * n:4 * n + 4, :],
                      B(4 * (1 - n), 0, 512).rearrange("p (g e) -> p g e", g=4), ALU.add, need=[(m_pool, "cdec")])
                dve.wait_ge(st_stored, 32 * it + 32 * H + 16)
                s("cp", copy, st_out[:, NB, :], B(1, 0, P))
                s("fg", tt, fac[:, :], fac[:, :], gate[:, :], ALU.mult, need=[(m_act, "rs")])
                s("mixf", stt, mixf[:, :], hm[:, :], norms[:, bass.ds(64 + it, 1)], fac[:, :], ALU.mult, ALU.mult)
                s("mixlo", tt, mix_lo[:, bass.ds(it, 1), :].rearrange("p o t -> p (o t)"), mixf[:, :],
                  mix_hi[:, bass.ds(it, 1), :].rearrange("p o t -> p (o t)").bitcast(F32), ALU.subtract, need=[(m_act, "mixhi")])
            dve.wait_ge(pads_ready, H + 1)
            with dve.Fori(0, H) as it:
                mlstm(it)

            s = runner(tail_v, 0)
            for n in range(6):
                s(f"c{n}", copy, conv_back[:, 512 * n:512 * n + 512], psum[0:NG * 3, 6 + n % 2, 0:512], need=[(tail, f"c{n}")])
            s("n", copy, k_tok[0:NG * H, 0, :], psum[0:NG * H, 6, 0:P], need=[(tail, "n")])

            dve.wait_ge(lo_pool, U_O)
            dve.sem_inc(lo_done, U_O - U_G - 3)
            with dve.Fori(0, KT // 4) as it:
                for i in range(4):
                    split_lo(dve, Unit(U_O, it, i + 1))

            s = runner(n_dve, 0)
            dve.wait_ge(x_back, 16)
            for k in range(KT):
                s(f"t{k}", stt, fsq[:, k % 2, :], acc_s[:, k, :], norms[:, KT + k:KT + k + 1], frb[:, :], ALU.mult, ALU.mult,
                  need=[(n_act, "r")])
                s(f"x{k}", tt, x2[:, k, :], x2[:, k, :], fsq[:, k % 2, :], ALU.add)
            for k in range(KT):
                if k >= 2:
                    dve.wait_ge(n_act.sem, n_act.at(0, f"uh{k - 2}"))
                s(f"ut{k}", stt, fsq[:, k % 2, :], x2[:, k, :], norms[:, 2 * KT + k:2 * KT + k + 1], frb[:, :], ALU.mult, ALU.mult,
                  need=[(n_act, "r2")])
                s(f"ul{k}", tt, u_lo[:, k, :], fsq[:, k % 2, :], u_hi[:, k, :].bitcast(F32), ALU.subtract,
                  need=[(n_act, f"uh{k}")])

            def gate_up(group, parity, base, it, i0, per=24):
                for j in range(4):
                    q = 4 * group + j
                    split_lo(dve, Unit(base, it, i0 + 2 * j + 1, per))
                    s = runner(f_dve, q)
                    s("add", ts, fe[:, :], fe[:, :], 1.0, None, ALU.add, need=[(f_act, "e")])
                    s("rec", dve.reciprocal, fe[:, :], fe[:, :])
                    s("s", tt, fe[:, :], fe[:, :], psum[:, 2 * (j % 2), 0:T], ALU.mult)
                    split_lo(dve, Unit(base, it, i0 + 2 * j + 2, per))
                    dve.wait_ge(unit_done, Unit(base, it, i0 + 2 * j + 1, per).u)
                    s("h", tt, fh[:, :], fe[:, :], psum[:, 2 * (j % 2) + 1, 0:T], ALU.mult)
                    s("lo", tt, h_lo[:, parity, j, :], fh[:, :], h_hi[:, parity, j, :].bitcast(F32), ALU.subtract,
                      need=[(f_act, "hi")])

            def down(group, base, it, i0, per=24, last=False):
                for n in range(4):
                    if not (last and n == 3):
                        split_lo(dve, Unit(base, it, i0 + n + 1, per))
                    dve.wait_ge(unit_done, Unit(base, it, i0 + n, per).u)
                    dve.wait_ge(acc_zero, 1)
                    dve.wait_ge(added.sem, added.before(group, str(n)))
                    dve.tensor_tensor(acc_s[:, 4 * n:4 * n + 4, :], acc_s[:, 4 * n:4 * n + 4, :], psum[:, 4:8, 0:T],
                                      ALU.add).then_inc(*added.step(str(n)))
            gate_up(0, 0, U_F, 0, 0)
            with dve.Fori(0, FG // 2) as it:
                for half in range(2):
                    gate_up(2 * it + 1 + half, 1 - half, U_F + 8, it, 12 * half)
                    down(2 * it + half, U_F + 8, it, 12 * half + 8)
            down(FG - 1, U_END - 4, 0, 0, last=True)

            s = runner(n_dve, 0)
            for k in range(KT):
                s(f"ft{k}", stt, fsq[:, k % 2, :], acc_s[:, k, :], norms[:, 3 * KT + k:3 * KT + k + 1], frb[:, :], ALU.mult, ALU.mult,
                  need=[(n_act, "r3")])
                s(f"fx{k}", tt, acc_s[:, k, :], x2[:, k, :], fsq[:, k % 2, :], ALU.add)


INPUTS = ("x_prompt", "x_sample", "state_mlstm_C", "state_mlstm_n", "state_mlstm_m", "state_gdn_S", "state_gdn_conv",
          "meta_tokens", "norm_pre_mix", "norm_post_mix", "norm_pre_ffn", "norm_post_ffn", "w_in", "mlstm_b_i", "mlstm_b_f",
          "mlstm_norm", "gdn_conv_w", "gdn_A_log", "gdn_dt_bias", "gdn_norm", "w_out", "w_gate_up", "w_down")
OUTPUTS = (("y_p", (1, SEQ, D)), ("y_s", (NB, DEC, D)),
           ("p_C", (1, 1, H, P, P)), ("p_n", (1, 1, H, P)), ("p_m", (1, 1, H)), ("p_S", (1, 1, H, P, P)), ("p_conv", (1, 1, 3, 3 * W1)),
           ("s_C", (1, NB, H, P, P)), ("s_n", (1, NB, H, P)), ("s_m", (1, NB, H)), ("s_S", (1, NB, H, P, P)),
           ("s_conv", (1, NB, 3, 3 * W1)))


def kernel(**inputs):
    import concourse.bacc as bacc
    from concourse.bass_utils import run_bass_kernel_spmd

    nc = bacc.Bacc("TRN2", target_bir_lowering=False, num_devices=1)
    table, _, joins, scan_mask = constant_tables()
    arrays = {name: np.ascontiguousarray(inputs[name]) for name in INPUTS}
    arrays |= {"table": table, "joins": joins, "scan_mask": scan_mask}
    A = {name: nc.dram_tensor(f"in_{name}", a.shape, mybir.dt.from_np(a.dtype), kind="ExternalInput").ap()
         for name, a in arrays.items()}
    O = {name: nc.dram_tensor(f"out_{name}", shape, F32, kind="ExternalOutput").ap() for name, shape in OUTPUTS}
    build_layer(nc, A, O)
    r = run_bass_kernel_spmd(nc, [{f"in_{k}": v for k, v in arrays.items()}], core_ids=[0])
    return tuple(r.results[0][f"out_{name}"] for name, _ in OUTPUTS)
```

```python
from contextlib import ExitStack

import numpy as np

import concourse.bass as bass
from concourse import mybir

F32 = mybir.dt.float32
F32R = mybir.dt.float32r
U8 = mybir.dt.uint8
ALU = mybir.AluOpType
ACT = mybir.ActivationFunctionType

P = 128
D = 2048
KT = D // P
H = 8
NB, DEC = 8, 4
META, SEQ = 16, 256
NP = META + SEQ
T = NP + NB * DEC
TP = 384
T2 = T - 2 * P
P2 = NP - 2 * P
NG = NB + 1
W1 = H * P
IN_COLS = 8 * W1 + 4 * H
GDN_COL = 4 * W1 + 2 * H
FF = 5632
FG = FF // 512
TAPS = 4
DEC0 = NP + TAPS - 1
GW = DEC + TAPS - 1
XW = DEC0 + NB * GW
YW = XW - (TAPS - 1)
EPS = 1e-6
QS = float(P) ** -0.5
NEG = -1e30
EXP_LN_SET = 6
LEVELS = 7
TILE = [(0, 0, P), (1, P, P), (2, 2 * P, T2)]


def constant_tables():
    pos = np.arange(TP)
    group = np.where(pos < NP, NB, (pos - NP) // DEC)
    group[T:] = 99
    j = np.arange(P)
    cols = {}
    cols["ident"] = np.eye(P)
    cols["ones"] = np.ones((P, P))
    cols["mean"] = np.full((P, P), 1.0 / P)

    def cap(tile, toks):
        a = tile * P + j
        ok = (toks[None, :] >= a[:, None]) & (group[toks][None, :] == group[a][:, None]) & (a[:, None] < T)
        return np.where(ok, 0.0, NEG)
    cols["cap_g"] = np.concatenate([cap(t, np.arange(s, s + n)) for t, s, n in TILE], 1)
    cols["cap_m"] = np.concatenate([cap(0, np.arange(NP)), cap(1, np.arange(P, NP)), cap(2, np.arange(2 * P, T))], 1)
    cols["neg_strict"] = -np.concatenate([1.0 - np.eye(P)[:, :n] for _, _, n in TILE], 1)
    g2 = group[2 * P + j]
    cols["gmask"] = (g2[:, None] == np.arange(NG)[None, :]) * 1.0
    cols["gmask_rows"] = np.broadcast_to((np.arange(NG)[:, None] == g2[None, :T2]).reshape(-1) * 1.0, (P, NG * T2))
    at, out = {}, []
    n = 0
    for k, v in cols.items():
        at[k] = (n, n + v.shape[1])
        n += v.shape[1]
        out.append(v)
    joins = []
    for lower in (True, False):
        for lv in range(LEVELS):
            s = 1 << lv
            r, c = j[:, None], j[None, :]
            m = (r // (2 * s) == c // (2 * s)) & (r // s % 2 == 1) & (c // s % 2 == 0)
            m = m if lower else m.T
            joins.append(np.concatenate([m[:, :n] for _, _, n in TILE], 1))
    start = np.zeros(T)
    start[0] = 1
    start[NP::DEC] = 1
    chunk = start.copy()
    chunk[[P, 2 * P]] = 1
    scan = np.stack([np.broadcast_to(1 - start, (H, T)), np.broadcast_to(1 - chunk, (H, T))], 1)
    return (np.concatenate(out, 1).astype(np.float32), at, np.stack(joins, 1).astype(np.float32),
            np.ascontiguousarray(scan).astype(np.float32))


_, CONST_AT, _, _ = constant_tables()
CONST_W = max(b for _, b in CONST_AT.values())


class Affine:

    def __init__(self, reg, mul, add):
        self.reg, self.mul, self.add = reg, mul, add

    def __mul__(self, n):
        return Affine(self.reg, self.mul * n, self.add * n)

    def __add__(self, n):
        return Affine(self.reg, self.mul, self.add + n)


def value(x):
    return x.reg * x.mul + x.add if isinstance(x, Affine) else x


class Steps:

    def __init__(self, sem, names):
        self.sem, self.names, self.done = sem, names.split(), 0
        self.n = len(self.names)

    def at(self, it, name):
        return value(it * self.n + (self.n + self.names.index(name) + 1))

    def before(self, it, name):
        return value(it * self.n + (self.n + self.names.index(name)))

    def prev(self, it, name):
        return it * self.n + (self.names.index(name) + 1)

    def skip(self, eng, it, names):
        eng.wait_ge(self.sem, self.before(it, names[0]))
        eng.sem_inc(self.sem, len(names))
        for name in names:
            self.step(name)

    def step(self, name):
        assert self.names[self.done % self.n] == name, (name, self.names[self.done % self.n])
        self.done += 1
        return self.sem, 1


def build_layer(nc, A, O):
    with ExitStack() as ctx:
        ctx.enter_context(nc.allow_non_contiguous_dma(reason="a few short columns"))

        def sb(name, shape, dt=F32, c=ctx):
            return c.enter_context(nc.sbuf_tensor(name, shape, dt))

        def sem(name):
            return ctx.enter_context(nc.semaphore(name))

        x_spill = nc.dram_tensor("x_spill", (P, KT, T), F32, kind="Internal").ap()

        raw = sb("raw", [P, 2, KT, P])
        whi = [sb(f"whi{i}", [P, KT, P], F32R) for i in range(2)]
        wlo = [sb(f"wlo{i}", [P, KT, P], F32R) for i in range(2)]
        u_hi, u_lo = sb("u_hi", [P, KT, T], F32R), sb("u_lo", [P, KT, T], F32R)
        first = ExitStack()
        join_masks = sb("join_masks", [P, 2 * LEVELS, T], F32, first)
        first.close()
        late = ExitStack()
        fs16 = sb("fs16", [P, KT, T], F32, late)
        late.close()
        mix_hi, mix_lo = sb("mix_hi", [P, KT, T], F32R), sb("mix_lo", [P, KT, T], F32R)
        cst = sb("cst", [P, CONST_W])
        joins = sb("joins", [P, 2 * LEVELS, T], U8)
        norms = sb("norms", [P, 80])
        eps_c = sb("eps_c", [P, 3])
        sel = sb("sel", [H, P])
        rows_m = sb("rows_m", [H, 2 * T + NB * DEC])
        rows_g = sb("rows_g", [H, 3 * T])
        m8 = sb("m8", [H, NB])
        bias8 = sb("bias8", [H, 4])
        mp = sb("mp", [H, NB])
        decay = sb("decay", [H, 1])
        ssum = sb("ssum", [P, 4])
        cols = sb("cols", [P, 3, 6, H])

        def C(name, rows=P):
            a, b = CONST_AT[name]
            return cst[0:rows, a:b]
        ident, ones, mean = C("ident"), C("ones"), C("mean")

        mixers = ExitStack()
        m_ = lambda name, shape, dt=F32: sb(name, shape, dt, mixers)
        stage = m_("stage", [P, 3, XW])
        stage_z = m_("stage_z", [P, T])
        convw = m_("convw", [P, 96])
        conv_in = m_("conv_in", [P, 3, H, NB * 3])
        conv_out = m_("conv_out", [P, 3, H, NG * 3])
        n_in = m_("n_in", [P, NB * H])
        n_out = m_("n_out", [P, NG, H])
        st_in = m_("st_in", [P, NB, P])
        st_out = m_("st_out", [P, NG, P])
        vm = m_("vm", [T2, NG, P])
        kn = m_("kn", [P, TP])
        qn = m_("qn", [P, T])
        dec = m_("dec", [P, T])
        k_tok = m_("k_tok", [P, 3, P])
        v_tok = m_("v_tok", [P, 3, P])
        fac = m_("fac", [P, T])
        gate = m_("gate", [P, T])
        mixf = m_("mixf", [P, T])
        sq = m_("sq", [P, 2, T])
        dcs = m_("dcs", [P, 2 + NB])
        only_g = ExitStack()
        g_ = lambda name, shape, dt=F32: sb(name, shape, dt, only_g)
        y = g_("y", [P, 3, YW])
        cs = g_("cs", [P, 3, TP])
        kb = g_("kb", [P, T])
        qeg = g_("qeg", [P, T])
        decn = g_("decn", [P, T])
        nat = g_("nat", [P, TP])
        pb = g_("pb", [P, TP])
        tinv, uinv = g_("tinv", [P, 3, P]), g_("uinv", [P, 3, P])
        kh_tok = g_("kh_tok", [P, 3, P])
        nkd = g_("nkd", [P, T])
        nkdm = g_("nkdm", [P, NG, T2])
        wv = g_("wv", [P, 3, P])
        s_chunk = g_("s_chunk", [P, 2, P])
        only_g.close()
        only_m = ExitStack()
        n_ = lambda name, shape, dt=F32: sb(name, shape, dt, only_m)
        sc_e = n_("sc_e", [P, 464])
        sc_p = n_("sc_p", [P, 464])
        vpad = n_("vpad", [P, TP])
        qi = n_("qi", [P, NB * DEC])
        nq = n_("nq", [P, NB * DEC])
        nm = n_("nm", [P, NB])
        hm = n_("hm", [P, T])
        only_m.close()

        x_c = ExitStack()
        x_ = lambda name, shape, dt=F32: sb(name, shape, dt, x_c)
        xtok = x_("xtok", [P, 3, D])
        x_out = x_("x_out", [P, 3, T])
        x_c.close()
        row_c = ExitStack()
        r_ = lambda name, shape, dt=F32: sb(name, shape, dt, row_c)
        gates = r_("gates", [4 * H, T])
        yf = r_("yf", [H, 2, T])
        la = r_("la", [H, 2, T])
        scan_m = r_("scan_m", [H, 2, T])
        li = r_("li", [H, T])
        b_row = r_("b_row", [H, T])
        m_row = r_("m_row", [H, T])
        col_src = r_("col_src", [H, 6, TP])
        row_c.close()
        tail_c = ExitStack()
        conv_back = sb("conv_back", [NG * 3, 3 * W1], F32, tail_c)
        tail_c.close()
        mixers.close()
        ffn = ExitStack()
        f_ = lambda name, shape, dt=F32: sb(name, shape, dt, ffn)
        x2 = f_("x2", [P, KT, T])
        acc_s = f_("acc_s", [P, KT, T])
        h_hi, h_lo = f_("h_hi", [P, 2, 4, T], F32R), f_("h_lo", [P, 2, 4, T], F32R)
        fe, fs, fh, frb = (f_(name, [P, T]) for name in ("fe", "fs", "fh", "frb"))
        fsq = f_("fsq", [P, 2, T])
        ffn.close()

        conv_rows = [vm[0:NB * 3].rearrange("p g e -> p (g e)")[:, 0:W1],
                     st_out[0:NB * 3].rearrange("p g e -> p (g e)")[:, 0:W1],
                     st_in[0:NB * 3].rearrange("p g e -> p (g e)")[:, 0:W1]]
        norm_rows = k_tok[0:80, 0, :]
        tap_rows = k_tok[0:96, 1, :]
        n_rows = k_tok[0:NB * H, 2, :]

        psum = ctx.enter_context(nc.psum_tensor("psum", [P, 8, 512], F32))

        def B(i, a=0, b=T):
            return psum[:, 2 + i, a:b]

        raw_in = [sem("raw_in0"), sem("raw_in1")]
        hi_done, lo_done = sem("hi_done"), sem("lo_done")
        lo_pool = sem("lo_pool")
        unit_done = sem("unit_done")
        evac_done = sem("evac_done")
        const_in, small_in, x_in, conv_rows_in = sem("const_in"), sem("small_in"), [sem(f"x_in{t}") for t in range(3)], sem("conv_rows_in")
        gates_in = sem("gates_in")
        spill_done = [sem(f"spill_done{i}") for i in range(3)]
        m_out = sem("m_out")
        pads_ready = sem("pads_ready")
        st_loaded, st_stored = sem("st_loaded"), sem("st_stored")
        x_back, rows_out, y_out = sem("x_back"), sem("rows_out"), [sem("y_out0"), sem("y_out1")]
        rows_in, joins_in = sem("rows_in"), sem("joins_in")
        acc_zero = sem("acc_zero")
        join_turn = sem("join_turn")
        tail = Steps(sem("tail"), "c0 c1 c2 c3 c4 c5 n")
        tail_v = Steps(sem("tail_v"), "c0 c1 c2 c3 c4 c5 n")
        y_tok = raw[:, :, 0:12, :].rearrange("p b (t k) n -> p b t k n", t=3)

        U_G, U_M = 4, 4 + 4 * H
        U_O = U_M + 4 * H
        U_F = U_O + KT
        U_END = U_F + 12 * FG

        SPLIT_AT, CONV_AT = 3, 8

        g_pe = Steps(sem("g_pe"), "ss kk tr l0 " + " ".join(f"p{i} q{i}" for i in range(1, LEVELS))
                     + " nkd w0 s1 w1 s2 w2 o st ms bc")
        g_act = Steps(sem("g_act"), "ln rs dec_exp vb0 vb1 vb2 z0 z1 z2 p1 p2 p3 p4 e0p e0d e0l e0s p5 p6"
                      + " nkd e1p e1d e1l e1s w0 w1 w2 e2p e2d e2l e2s osq esq oln ors mixhi")
        g_dve = Steps(sem("g_dve"), "e0 e1 e2 kn kb qn qeg d1 d2 d3 nat t0 u0 qkd kb0 kb1 kb2 t1 u1 kh0 kh1 kh2 gate"
                      + " t2 u2 c0w0 c0w1 t3 u3 c0w2 c0w3 t4 u4 c1w0 c1w1 t5 u5 c1w2 c1w3 u6"
                      + " nkdm s1 c2w0 c2w1 s2 c2w2 c2w3 cs_p cs_d so0 so1 sp omul omix mixlo")
        g_pool = Steps(sem("g_pool"), "decn sdec save_p save_d sel wm ti ui")
        m_pe = Steps(sem("m_pe"), "bc tr sc num den st ms")
        m_act = Steps(sem("m_act"), "q k vp oe v exp absd hsq ln rs mixhi")
        m_dve = Steps(sem("m_dve"), "o1 gate e0 e1 e2 kw0 kw1 kw2 pm qi nq dcp dmax drec h nm na np co0 co1 cp fg mixf mixlo")
        m_pool = Steps(sem("m_pool"), "sel vm cdec")
        o_pe, o_act = Steps(sem("o_pe"), "ms"), Steps(sem("o_act"), "copy sq")
        f_act, f_dve = Steps(sem("f_act"), "e l s hi"), Steps(sem("f_dve"), "g a u h lo")
        half_done = sem("half_done")
        added = Steps(sem("added"), "0a 0b 1a 1b 2a 2b 3a 3b")
        each = lambda *names: " ".join(f"{x}{k}" for k in range(KT) for x in names)
        skew = lambda early, late: " ".join([f"{early}{k}" for k in range(1)] + [x for k in range(1, KT) for x in
                                            (f"{early}{k}", f"{late}{k - 1}")] + [f"{late}{KT - 1}"])
        a_pe = Steps(sem("a_pe"), "norms rb " + " ".join(f"x{k}" + (" conv" if k == CONV_AT else "") for k in range(KT)) + " sel cols bc")
        a_act = Steps(sem("a_act"), "ss0 ss1 ss2 ln r " + skew("xo", "uh") + " gates ea bexp abs aexp aln iexp em eg wl kh " + " ".join(f"e{c}{x}" for c in range(3) for x in "pdls") + " esq")
        a_dve = Steps(sem("a_dve"), "ones norms convw n_in dg0 dg1 dg2 rb " + skew("ut", "ul") + " ci0 ci1"
                      + " li yf0 yf1 b1 b2 lf sp lg bsc gsc c mx0 t8 mx1 ng0 ng1 msc r it wl0 wl1 ngg kh0 kh1 kh2 kh3 nb bc cols " + " ".join(f"c{c}w{i}" for c in range(3) for i in range(TAPS)) + " cs_p cs_d")
        a_pool = Steps(sem("a_pool"), "z0 z1 z2 joins z3 z4 z5 sel ti ui")
        n_pe = Steps(sem("n_pe"), "ms2 ffn " + each("y"))
        n_act = Steps(sem("n_act"), "ln r " + each("sq", "uh") + " ln2 r2 " + each("fq") + " ln3 r3 " + each("yc"))
        n_dve = Steps(sem("n_dve"), " ".join((f"t{k} " if k < KT else "") + (f"ul{k - 2}" if k >= 2 else "") for k in range(KT + 2))
                      + " " + each("ft"))
        n_pool = Steps(sem("n_pool"), each("x") + " " + each("fx"))

        class Unit:
            def __init__(self, base, it, i, per=4):
                self.u = base + per * it + i
                self.landed = 16 * ((base + i) // 2 - 1) + 8 * per * it
                self.slot = i % 2

        w_in_v = A["w_in"][0].rearrange("(k p) n -> p k n", p=P)
        w_out_v = A["w_out"][0].rearrange("(k p) n -> p k n", p=P)
        w_gu_v = A["w_gate_up"][0].rearrange("(k p) n -> p k n", p=P)
        w_dn_v = A["w_down"][0].rearrange("(k p) n -> p k n", p=P)

        def load_unit(eng, w, view, split=lo_done):
            eng.wait_ge(split, w.u - 2)
            dst = raw[:, w.slot]
            if view.shape[1] == 4:
                dst = dst.rearrange("p (k m) n -> p k (m n)", k=4)
            eng.dma_start(dst, view).then_inc(raw_in[w.slot], 16)

        def split_hi(act, w):
            act.wait_ge(raw_in[w.slot], w.landed)
            act.wait_ge(unit_done, w.u - 2)
            act.activation(whi[w.slot][:, :, :], raw[:, w.slot], ACT.Copy).then_inc(hi_done, 1)

        def split_lo(eng, w, done=lo_done):
            eng.wait_ge(hi_done, w.u)
            eng.tensor_tensor(wlo[w.slot][:, :, :], raw[:, w.slot], whi[w.slot][:, :, :].bitcast(F32),
                              ALU.subtract).then_inc(done, 1)

        def products(pe, out, pairs, first, last):
            for n, (a, b, xh, xl) in enumerate(pairs):
                pe.matmul(out, a, xh, start=(first and n == 0), stop=False)
                pe.matmul(out, a, xl, start=False, stop=False)
                ins = pe.matmul(out, b, xh, start=False, stop=(last and n == len(pairs) - 1))
            return ins

        def tiles(w, kts, xh, xl):
            return [(whi[w.slot][:, k, :], wlo[w.slot][:, k, :], xh[:, k, :], xl[:, k, :]) for k in kts]

        PARTS = 8

        def unit_part(pe, w, part, xh, xl, split=lo_pool):
            if part == 0:
                pe.wait_ge(split, w.u)
                pe.wait_ge(evac_done, w.u - 2)
            n = KT // PARTS
            ins = products(pe, psum[:, w.slot, 0:T], tiles(w, range(part * n, part * n + n), xh, xl),
                           first=(part == 0), last=(part == PARTS - 1))
            if part == PARTS - 1:
                ins.then_inc(unit_done, 1)

        SLOT_G = dict(ss=0, kk=5, tr=6, l0=7, nkd=20, w0=21, s1=22, w1=24, s2=25, w2=26, o=27, st=28, ms=30, bc=31)
        for n in range(1, LEVELS):
            SLOT_G[f"p{n}"], SLOT_G[f"q{n}"] = 6 + 2 * n, 7 + 2 * n
        SLOT_M = dict(bc=1, tr=3, sc=5, num=11, den=13, st=16, ms=22)

        def group_cols(t, a=NP, w=DEC):
            return t[:, a:a + NB * w].rearrange("p (b w) -> p b w", w=w)

        def conv_groups(t):
            t = t[:, DEC0:DEC0 + (NB - 1) * GW + DEC]
            return bass.AP(t.tensor, t.offset, [list(t.ap[0]), [GW, NB], [1, DEC]])

        def stage_dst(i, kind):
            if i == 3:
                return [(stage_z[:, :], (0, T))]
            if kind == "m":
                return [(stage[:, i, 0:T], (0, T))]
            return [(stage[:, i, TAPS - 1:DEC0], (0, NP)),
                    (stage[:, i, DEC0:XW].rearrange("p (b w) -> p b w", w=GW)[:, :, TAPS - 1:GW], (NP, T))]

        def evacuate(act, w, i, kind):
            act.wait_ge(unit_done, w.u)
            dst = stage_dst(i, kind)
            for n, (out, (a, b)) in enumerate(dst):
                src = psum[:, w.slot, a:b]
                if len(out.shape) == 3:
                    src = src.rearrange("p (b w) -> p b w", w=DEC)
                ins = act.activation(out, src, ACT.Copy)
                if n == len(dst) - 1:
                    ins.then_inc(evac_done, 1)

        block = ctx.enter_context(nc.Block())

        @block.sync
        def _(sp):
            xp, xs, meta = A["x_prompt"][0], A["x_sample"].rearrange("b t d -> (b t) d"), A["meta_tokens"]
            sp.dma_start(xtok[0:META, 0, :], meta).then_inc(x_in[0], 16)
            sp.dma_start(xtok[META:P, 0, :], xp[0:P - META, :]).then_inc(x_in[0], 16)
            sp.dma_start(xtok[:, 1, :], xp[P - META:2 * P - META, :]).then_inc(x_in[1], 16)
            sp.dma_start(xtok[0:P2, 2, :], xp[2 * P - META:SEQ, :]).then_inc(x_in[2], 16)
            sp.dma_start(xtok[P2:T2, 2, :], xs).then_inc(x_in[2], 16)
            sp.dma_start(raw[:, 1, :, 0:2 * H], w_in_v[:, :, 4 * W1:4 * W1 + 2 * H]).then_inc(gates_in, 16)
            sp.dma_start(raw[:, 1, :, 2 * H:4 * H], w_in_v[:, :, IN_COLS - 2 * H:IN_COLS]).then_inc(gates_in, 16)

            def head_units(base, col, it, split):
                for i in range(4):
                    load_unit(sp, Unit(base, it, i), w_in_v[:, :, bass.ds(col + i * W1 + it * P, P)], split(i))

            def out_units(it, split):
                for i in range(4):
                    load_unit(sp, Unit(U_O, it, i), w_out_v[:, :, bass.ds((4 * it + i) * P, P)], split(i))
            head_units(U_G, GDN_COL, 0, lambda i: lo_done)
            head_units(U_G, GDN_COL, 1, lambda i: lo_done if i < 2 else lo_pool)
            with sp.Fori(2, H) as it:
                head_units(U_G, GDN_COL, it, lambda i: lo_pool)
            with sp.Fori(0, H) as it:
                head_units(U_M, 0, it, lambda i: lo_pool)
            out_units(0, lambda i: lo_pool if i < 3 else lo_done)
            with sp.Fori(1, KT // 4) as it:
                out_units(it, lambda i: lo_done)

            def gate_up(group, base, it, i0, per=24):
                for j in range(4):
                    for half in range(2):
                        load_unit(sp, Unit(base, it, i0 + 2 * j + half, per),
                                  w_gu_v[:, :, bass.ds(half * FF + group * 512 + j * P, P)])

            def down(group, base, it, i0, per=24):
                for n in range(4):
                    load_unit(sp, Unit(base, it, i0 + n, per),
                              w_dn_v[:, bass.ds(4 * group, 4), n * 512:n * 512 + 512])
            gate_up(0, U_F, 0, 0)
            with sp.Fori(0, FG // 2) as it:
                gate_up(2 * it + 1, U_F + 8, it, 0)
                down(2 * it, U_F + 8, it, 8)
                gate_up(2 * it + 2, U_F + 8, it, 12)
                down(2 * it + 1, U_F + 8, it, 20)
            down(FG - 1, U_END - 4, 0, 0)
            for g in range(KT // 4):
                b, c = g % 2, slice(512 * g, 512 * g + 512)
                sp.wait_ge(n_act.sem, n_act.at(0, f"yc{4 * g + 3}"))
                yp, ys = O["y_p"][0], O["y_s"].rearrange("b t d -> (b t) d")
                for rows, t, dst in ((slice(META, P), 0, yp[0:P - META, c]), (slice(0, P), 1, yp[P - META:2 * P - META, c]),
                                     (slice(0, P2), 2, yp[2 * P - META:SEQ, c]), (slice(P2, T2), 2, ys[:, c])):
                    sp.dma_start(dst, y_tok[rows, b, t, :, :].rearrange("p k n -> p (k n)")).then_inc(y_out[b], 16)
            for b in range(2):
                sp.wait_ge(y_out[b], 64 * (KT // 8))

        @block.gpsimd
        def _(pool):
            for c in (a_pool, g_pool, m_pool, n_pool):
                pool.sem_inc(c.sem, c.n)
            pool.sem_inc(lo_pool, U_G + 3)
            def pads(h):
                pool.wait_ge(const_in, 16)
                pool.tensor_copy(stage[:, :, DEC0:XW].rearrange("p c (b w) -> p c b w", w=GW)[:, :, :, 0:TAPS - 1],
                                 conv_in[:, :, bass.ds(h, 1), :].rearrange("p c o (b r) -> p (c o) b r", r=3)
                                 ).then_inc(pads_ready, 1)
            for n, part in enumerate((stage[:, :, 0:TAPS - 1], kn[:, T:TP])):
                pool.memset(part, 0.0).then_inc(*a_pool.step(f"z{n}"))
            for k in range(KT):
                pool.wait_ge(a_act.sem, a_act.at(0, f"xo{k}"))
                pool.dma_start(x_spill[:, k, :], x_out[:, k % 3, :]).then_inc(spill_done[k % 3], 16)
            pool.memset(col_src[:, :, :], 0.0).then_inc(*a_pool.step("z2"))
            pool.dma_start(scan_m[:, :, :], A["scan_mask"]).then_inc(st_stored, 16)
            pool.wait_ge(joins_in, 16)
            pool.tensor_copy(joins[:, :, :], join_masks[:, :, :]).then_inc(*a_pool.step("joins"))
            pool.wait_ge(a_dve.sem, a_dve.at(0, "ci1"))
            pads(0)
            pool.wait_ge(a_dve.sem, a_dve.at(0, "cols"))
            pool.wait_ge(a_act.sem, a_act.at(0, "kh"))
            for n, part in enumerate((cs[:, :, T:TP], nat[:, T:TP], pb[:, T:TP])):
                pool.memset(part, 0.0).then_inc(*a_pool.step(f"z{3 + n}"))
            pool.dma_start(O["p_m"].rearrange("l b h -> h (l b)"), m_row[:, NP - 1:NP]).then_inc(m_out, 16)
            pool.dma_start(O["s_m"][0].rearrange("b h -> h b"), group_cols(m_row)[:, :, DEC - 1]).then_inc(m_out, 16)

            C_v = A["state_mlstm_C"][0].rearrange("b h d e -> h d b e")
            S_v = A["state_gdn_S"][0].rearrange("b h d e -> h d b e")
            CO_s, CO_p = O["s_C"][0].rearrange("b h d e -> h d b e"), O["p_C"][0].rearrange("b h d e -> h d b e")
            SO_s, SO_p = O["s_S"][0].rearrange("b h d e -> h d b e"), O["p_S"][0].rearrange("b h d e -> h d b e")

            def of(view, h):
                return view[bass.ds(h, 1)].rearrange("h d b e -> d (h b) e")

            def load_state(view, h):
                pool.dma_start(st_in[:, :, :], of(view, h)).then_inc(st_loaded, 16)

            def store_state(s_view, p_view, h):
                pool.dma_start(of(s_view, h), st_out[:, 0:NB, :]).then_inc(st_stored, 16)
                pool.dma_start(of(p_view, h), st_out[:, NB:NG, :]).then_inc(st_stored, 16)
            load_state(S_v, 0)
            pool.wait_ge(a_dve.sem, a_dve.at(0, "c2w3"))

            split_lo(pool, Unit(U_G, 0, 4), lo_pool)

            def select(head, counter, step):
                pool.wait_ge(const_in, 16)
                pool.tensor_copy(sel[:, :], ident[0:H, bass.ds(head, 1)].to_broadcast([H, P])).then_inc(*counter.step(step))
            select(0, a_pool, "sel")
            pool.wait_ge(m_out, 32)

            def identities(counter):
                for name, buf in (("ti", tinv), ("ui", uinv)):
                    pool.tensor_tensor(buf[:, :, :], ident.unsqueeze(1).to_broadcast([P, 3, P]),
                                       ident.unsqueeze(1).to_broadcast([P, 3, P]), ALU.mult).then_inc(*counter.step(name))
            identities(a_pool)

            def gdn(it, last):
                nxt = [Unit(U_G, it, 4 + i) for i in range(5)]
                pool.wait_ge(g_act.sem, g_act.at(it, "dec_exp"))
                pool.wait_ge(g_dve.sem, g_dve.before(it, "e0"))
                pool.tensor_tensor(decn[:, :], dec[:, :], C("neg_strict"), ALU.mult).then_inc(*g_pool.step("decn"))
                split_lo(pool, nxt[1], lo_pool)
                if not last:
                    pool.wait_ge(g_dve.sem, g_dve.prev(it, "c2w3"))
                    pads(it + 1)
                pool.wait_ge(st_loaded, 16 * (it + 1))
                pool.wait_ge(g_dve.sem, g_dve.at(it, "d3"))
                pool.wait_ge(st_stored, 32 * it + 16)
                pool.tensor_tensor(st_out[:, 0:NB, :], st_in[:, :, :],
                                   dcs[:, 2:2 + NB].unsqueeze(2).to_broadcast([P, NB, P]), ALU.mult
                                   ).then_inc(*g_pool.step("sdec"))
                pool.wait_ge(evac_done, Unit(U_G, it, 2).u)
                pool.wait_ge(const_in, 16)
                pool.tensor_copy(conv_out[:, :, bass.ds(it, 1), 3 * NB:].rearrange("p c o r -> p (c o) r"),
                                 stage[:, :, DEC0 - 3:DEC0]).then_inc(*g_pool.step("save_p"))
                pool.wait_ge(const_in, 16)
                pool.tensor_copy(conv_out[:, :, bass.ds(it, 1), 0:3 * NB].rearrange("p c o (b r) -> p (c o) b r", r=3),
                                 stage[:, :, DEC0:XW].rearrange("p c (b w) -> p c b w", w=GW)[:, :, :, GW - 3:GW]
                                 ).then_inc(*g_pool.step("save_d"))
                if last:
                    g_pool.skip(pool, it, ["sel"])
                else:
                    select(it + 1, g_pool, "sel")
                split_lo(pool, nxt[2], lo_pool)
                split_lo(pool, nxt[3], lo_pool)
                pool.wait_ge(g_act.sem, g_act.at(it, "w2"))
                pool.tensor_tensor(vm[:, :, :], wv[0:T2, 2, :].unsqueeze(1).to_broadcast([T2, NG, P]),
                                   C("gmask", T2).unsqueeze(2).to_broadcast([T2, NG, P]), ALU.mult
                                   ).then_inc(*g_pool.step("wm"))
                split_lo(pool, nxt[4], lo_pool)
                pool.wait_ge(g_pe.sem, g_pe.at(it, "o"))
                pool.wait_ge(g_pool.sem, g_pool.at(it, "sdec"))
                load_state(C_v, 0) if last else load_state(S_v, it + 1)
                if last:
                    g_pool.skip(pool, it, ["ti", "ui"])
                else:
                    identities(g_pool)
                pool.wait_ge(g_dve.sem, g_dve.at(it, "sp"))
                store_state(SO_s, SO_p, it)
            with pool.Fori(0, H - 1) as it:
                gdn(it, False)
            gdn(H - 1, True)
            pool.wait_ge(g_dve.sem, g_dve.at(H - 1, "mixlo"))
            pool.memset(vpad[:, T:TP], 0.0).then_inc(pads_ready, 1)

            def mlstm(it, last):
                split = (lambda i: None) if last else (lambda i: split_lo(pool, Unit(U_M, it, 4 + i), lo_pool))
                pool.wait_ge(m_pe.sem, m_pe.before(it, "bc"))
                pool.wait_ge(const_in, 16)
                pool.tensor_copy(sel[:, :], ident[0:H, bass.ds(it, 1)].to_broadcast([H, P])).then_inc(*m_pool.step("sel"))
                split(1)
                pool.wait_ge(m_act.sem, m_act.at(it, "v"))
                pool.wait_ge(m_pe.sem, m_pe.before(it, "bc"))
                pool.tensor_tensor(vm[:, :, :], v_tok[0:T2, 2, :].unsqueeze(1).to_broadcast([T2, NG, P]),
                                   C("gmask", T2).unsqueeze(2).to_broadcast([T2, NG, P]), ALU.mult
                                   ).then_inc(*m_pool.step("vm"))
                split(2)
                pool.wait_ge(st_loaded, 16 * (it + H + 1))
                pool.wait_ge(m_dve.sem, m_dve.at(it, "dcp"))
                pool.wait_ge(st_stored, 32 * it + 32 * H + 16)
                pool.tensor_tensor(st_out[:, 0:NB, :], st_in[:, :, :],
                                   dcs[:, 0:NB].unsqueeze(2).to_broadcast([P, NB, P]), ALU.mult
                                   ).then_inc(*m_pool.step("cdec"))
                split(3)
                if not last:
                    pool.wait_ge(m_pe.sem, m_pe.at(it, "num"))
                    pool.wait_ge(m_pool.sem, m_pool.at(it, "cdec"))
                    load_state(C_v, it + 1)
                pool.wait_ge(m_dve.sem, m_dve.at(it, "cp"))
                store_state(CO_s, CO_p, it)
                split(4)
            with pool.Fori(0, H - 1) as it:
                mlstm(it, False)
            mlstm(H - 1, True)
            pool.wait_ge(tail_v.sem, tail_v.at(0, "c5"))
            pool.dma_start(O["s_conv"][0].rearrange("b r n -> (b r) n"), conv_back[0:3 * NB, :]).then_inc(rows_out, 16)
            pool.dma_start(O["p_conv"][0, 0], conv_back[3 * NB:3 * NG, :]).then_inc(rows_out, 16)
            pool.wait_ge(tail_v.sem, tail_v.at(0, "n"))
            pool.dma_start(O["s_n"][0].rearrange("b h d -> (b h) d"), k_tok[0:NB * H, 0, :]).then_inc(rows_out, 16)
            pool.dma_start(O["p_n"][0, 0], k_tok[NB * H:NG * H, 0, :]).then_inc(rows_out, 16)
            pool.wait_ge(st_stored, 64 * H + 16)
            pool.wait_ge(rows_out, 16 * 4)
            pool.wait_ge(m_act.sem, m_act.at(H - 1, "mixhi"))
            pool.wait_ge(m_dve.sem, m_dve.at(H - 1, "mixlo"))
            for i in range(3):
                pool.wait_ge(spill_done[i], 16 * len(range(i, KT, 3)))
            pool.dma_start(x2[:, :, :], x_spill).then_inc(x_back, 16)
            pool.wait_ge(x_back, 16)
            for k in range(KT):
                pool.wait_ge(n_dve.sem, n_dve.at(0, f"t{k}"))
                pool.tensor_tensor(x2[:, k, :], x2[:, k, :], fsq[:, k % 2, :], ALU.add).then_inc(*n_pool.step(f"x{k}"))
            pool.memset(acc_s[:, :, :], 0.0).then_inc(acc_zero, 1)
            for k in range(KT):
                pool.wait_ge(n_dve.sem, n_dve.at(0, f"ft{k}"))
                pool.tensor_tensor(acc_s[:, k, :], x2[:, k, :], fsq[:, k % 2, :], ALU.add).then_inc(*n_pool.step(f"fx{k}"))

        def to_unit(split, taken):
            at = [-1]

            def go(slot):
                while at[0] < min(slot // PARTS, 4):
                    at[0] += 1
                    if at[0] > 0:
                        taken(at[0] - 1)
                    if at[0] < 4:
                        split(at[0] + 1)
            return go

        @block.scalar
        def _(act):
            act.sem_inc(hi_done, 2)
            act.sem_inc(evac_done, 2)
            for c in (a_act, g_act, m_act, o_act, f_act, n_act):
                act.sem_inc(c.sem, c.n)
            act.add_instruction(mybir.InstLoadActFuncSet(name=nc.get_next_instruction_name(), act_func_set_id=EXP_LN_SET,
                                                         engine=mybir.EngineType.Activation))
            act.dma_start(cst[:, :], A["table"]).then_inc(const_in, 16)
            for n, name in enumerate(("norm_pre_mix", "norm_post_mix", "norm_pre_ffn", "norm_post_ffn")):
                act.dma_start(norm_rows[KT * n:KT * n + KT], A[name][0].rearrange("(k p) -> k p", p=P)).then_inc(small_in, 16)
            act.dma_start(norm_rows[64:72], A["mlstm_norm"][0]).then_inc(small_in, 16)
            act.dma_start(norm_rows[72:80], A["gdn_norm"][0]).then_inc(small_in, 16)
            act.dma_start(tap_rows, A["gdn_conv_w"][0].rearrange("w (c p) -> (w c) p", p=P)).then_inc(small_in, 16)
            act.dma_start(n_rows, A["state_mlstm_n"][0].rearrange("b h d -> (b h) d")).then_inc(small_in, 16)
            act.dma_start(join_masks[:, :, :], A["joins"]).then_inc(joins_in, 16)
            for n, name in enumerate(("mlstm_b_i", "mlstm_b_f", "gdn_dt_bias", "gdn_A_log")):
                act.dma_start(bias8[:, n:n + 1], A[name].rearrange("l h -> h l")).then_inc(rows_in, 16)
            act.dma_start(mp[:, :], A["state_mlstm_m"][0].rearrange("b h -> h b")).then_inc(rows_in, 16)
            for c in range(3):
                act.dma_start(conv_rows[c], A["state_gdn_conv"][0].rearrange("b r n -> (b r) n")[:, c * W1:c * W1 + W1]).then_inc(rows_in, 16)

            def a(name, out, in_, fn, need=(), **kw):
                for c, x in need:
                    act.wait_ge(c.sem, c.at(0, x))
                act.wait_ge(a_act.sem, a_act.before(0, name))
                act.activation(out, in_, fn, **kw).then_inc(*a_act.step(name))
            w0 = [Unit(U_G, 0, i) for i in range(5)]
            act.wait_ge(a_dve.sem, a_dve.at(0, "ones"))
            for t, _, n in TILE:
                act.wait_ge(x_in[t], 16 * (1 if t == 1 else 2))
                a(f"ss{t}", psum[0:n, 4:8, :].rearrange("p b c -> p (b c)"), xtok[0:n, t, :], ACT.Square,
                  accum_out=ssum[0:n, t:t + 1])
            a("ln", ssum[:, 0:3], ssum[:, 0:3], ACT.Ln, scale=1.0 / D, bias=eps_c[:, 0:1])
            a("r", ssum[:, 0:3], ssum[:, 0:3], ACT.Exp, scale=-0.5)
            for k in range(KT + 1):
                if k == SPLIT_AT:
                    act.wait_ge(gates_in, 32)
                    act.activation(whi[1][:, :, 0:4 * H], raw[:, 1, :, 0:4 * H], ACT.Copy).then_inc(hi_done, 1)
                    split_hi(act, w0[0])
                if k < KT:
                    if k >= 3:
                        act.wait_ge(spill_done[k % 3], 16 * (k // 3))
                        act.wait_ge(a_dve.sem, a_dve.at(0, f"ut{k - 3}"))
                    a(f"xo{k}", x_out[:, k % 3, :], psum[:, 2 + k % 4, 0:T], ACT.Copy, [(a_pe, f"x{k}")])
                if k >= 1:
                    a(f"uh{k - 1}", u_hi[:, k - 1, :], sq[:, (k - 1) % 2, :], ACT.Copy, [(a_dve, f"ut{k - 1}")])
            act.wait_ge(unit_done, 3)
            a("gates", gates[:, :], psum[0:4 * H, 1, 0:T], ACT.Copy)
            act.wait_ge(a_act.sem, a_act.at(0, "gates"))
            act.sem_inc(evac_done, 1)
            split_hi(act, w0[1])
            act.wait_ge(a_pool.sem, a_pool.at(0, "z0"))
            evacuate(act, w0[0], 0, "g")
            split_hi(act, w0[2])
            act.wait_ge(rows_in, 16 * 8)
            a("ea", decay[:, :], bias8[:, 3:4], ACT.Exp)
            a("bexp", rows_g[:, T:2 * T], psum[0:H, 5, 0:T], ACT.Exp, [(a_pe, "sel")], scale=-1.0)
            a("abs", la[:, :, :], yf[:, :, :], ACT.Abs, [(a_dve, "yf1")])
            a("aexp", la[:, :, :], la[:, :, :], ACT.Exp, scale=-1.0)
            a("aln", la[:, :, :], la[:, :, :], ACT.Ln, bias=eps_c[0:H, 1:2])
            evacuate(act, w0[1], 1, "g")
            split_hi(act, w0[3])
            a("iexp", rows_m[:, T:T + NB * DEC], rows_m[:, T:T + NB * DEC], ACT.Exp, [(a_dve, "it")])
            a("em", rows_m[:, T + NB * DEC:], m_row[:, :], ACT.Exp, [(a_dve, "msc")], scale=-1.0)
            a("eg", rows_g[:, 2 * T:], rows_g[:, 0:T], ACT.Exp, [(a_dve, "gsc")])
            a("wl", col_src[:, 1, 0:T], col_src[:, 1, 0:T], ACT.Exp, [(a_dve, "wl1")])
            a("kh", col_src[:, 5, 0:T], col_src[:, 5, 0:T], ACT.Exp, [(a_dve, "kh3")])
            act.wait_ge(a_act.sem, a_act.at(0, "kh"))
            evacuate(act, w0[2], 2, "g")
            split_hi(act, w0[4])
            evacuate(act, w0[3], 3, "g")

            def sigmoid(s, dv, c):
                one = eps_c[:, 1:2]
                s(f"e{c}p", cs[:, c, 0:NP], y[:, c, 0:NP], ACT.Exp, [(dv, f"c{c}w3")], scale=-1.0)
                s(f"e{c}d", group_cols(cs[:, c, :]), conv_groups(y[:, c, :]), ACT.Exp, scale=-1.0)
                s(f"e{c}l", cs[:, c, 0:T], cs[:, c, 0:T], ACT.Ln, bias=one)
                s(f"e{c}s", cs[:, c, 0:T], cs[:, c, 0:T], ACT.Exp, scale=-1.0)
            s0 = lambda name, out, in_, fn, need=(), **kw: a(name, out, in_, fn, need, **kw)
            for c in range(3):
                sigmoid(s0, a_dve, c)
            s0("esq", sq[:, :, :], cs[:, 0:2, 0:T], ACT.Square, [(a_dve, "cs_d")])

            def gdn(it, kind):
                early = kind == "g"
                nxt = [Unit(U_G, it, 4 + i) for i in range(5)]

                def taken(i):
                    if i < 3:
                        act.wait_ge(g_dve.sem, g_dve.prev(it, f"c{i}w3"))
                        act.wait_ge(g_pool.sem, g_pool.at(it, "save_d"))
                    else:
                        act.wait_ge(g_dve.sem, g_dve.at(it, "gate"))
                    evacuate(act, nxt[i], i, kind)
                go = to_unit(lambda i: split_hi(act, nxt[i]), taken)

                def s(name, out, in_, fn, need=(), slot=None, **kw):
                    for c, x in need:
                        act.wait_ge(c.sem, c.at(it, x))
                    act.wait_ge(g_act.sem, g_act.before(it, name))
                    act.activation(out, in_, fn, **kw).then_inc(*g_act.step(name))
                    if slot:
                        go(SLOT_G[slot])
                s("ln", sq[:, :, :], psum[:, 5:8:2, 0:T], ACT.Ln, [(g_pe, "ss")], bias=eps_c[:, 0:1])
                s("rs", sq[:, :, :], sq[:, :, :], ACT.Exp, scale=-0.5)
                s("dec_exp", dec[:, :], dec[:, :], ACT.Exp, [(g_dve, "e2")])
                go(0)
                for t in range(3):
                    s(f"vb{t}", v_tok[:, t, :], B(5, t * P, t * P + P), ACT.Copy, [(g_pe, "tr")], "tr",
                      scale=cols[:, t, 4, bass.ds(it, 1)])
                s("z0", gate[:, :], stage_z[:, :], ACT.Exp, scale=-1.0)
                s("z1", gate[:, :], gate[:, :], ACT.Ln, bias=eps_c[:, 1:2])
                s("z2", gate[:, :], gate[:, :], ACT.Exp, scale=-1.0)

                def next_sigmoid(c):
                    if early:
                        sigmoid(s, g_dve, c)
                    else:
                        g_act.skip(act, it, [f"e{c}{x}" for x in "pdls"])
                for lv in range(1, LEVELS):
                    s(f"p{lv}", pb[:, 0:T], B(1), ACT.Copy, [(g_pe, f"p{lv}")], f"p{lv}")
                    if lv == 4:
                        next_sigmoid(0)
                s("nkd", nkd[:, :], B(4), ACT.Copy, [(g_pe, "nkd")], "nkd")
                next_sigmoid(1)
                for t in range(3):
                    s(f"w{t}", wv[:, t, :], B(5, t * P, t * P + P), ACT.Copy, [(g_pe, f"w{t}")], f"w{t}")
                next_sigmoid(2)
                s("osq", fac[:, :], B(4), ACT.Square, [(g_pe, "o")], "o")
                if early:
                    s("esq", sq[:, :, :], cs[:, 0:2, 0:T], ACT.Square, [(g_dve, "cs_d")])
                else:
                    g_act.skip(act, it, ["esq"])
                s("oln", fac[:, :], B(5), ACT.Ln, [(g_pe, "ms")], "ms", bias=eps_c[:, 0:1])
                s("ors", fac[:, :], fac[:, :], ACT.Exp, scale=-0.5)
                go(4 * PARTS)
                s("mixhi", mix_hi[:, bass.ds(it + H, 1), :].rearrange("p o t -> p (o t)"), mixf[:, :], ACT.Copy, [(g_dve, "omix")])
            with act.Fori(0, H - 1) as it:
                gdn(it, "g")
            gdn(H - 1, "m")

            def mlstm(it, last):
                own = Unit(U_M, it, 3)
                nxt = [Unit(U_M, it, 4 + i) for i in range(5)]

                def taken(i):
                    act.wait_ge(m_act.sem, m_act.at(it, "oe"))
                    evacuate(act, nxt[i], i, "m")
                go = (lambda slot: None) if last else to_unit(lambda i: split_hi(act, nxt[i]), taken)

                def s(name, out, in_, fn, need=(), slot=None, **kw):
                    if slot:
                        go(SLOT_M[slot])
                    for c, x in need:
                        act.wait_ge(c.sem, c.at(it, x))
                    act.wait_ge(m_act.sem, m_act.before(it, name))
                    act.activation(out, in_, fn, **kw).then_inc(*m_act.step(name))
                go(0)
                act.wait_ge(evac_done, own.u)
                act.wait_ge(m_dve.sem, m_dve.before(it, "o1"))
                act.wait_ge(m_pe.sem, m_pe.before(it, "bc"))
                s("q", qn[:, :], stage[:, 0, 0:T], ACT.Copy, scale=QS)
                s("k", kn[:, 0:T], stage[:, 1, 0:T], ACT.Copy)
                s("vp", vpad[:, 0:T], stage[:, 2, 0:T], ACT.Copy)
                s("oe", gate[:, :], stage_z[:, :], ACT.Exp, scale=-1.0)
                act.wait_ge(m_pool.sem, m_pool.before(it, "sel"))
                s("v", v_tok[:, :, :].rearrange("p t e -> p (t e)"), B(4, 0, TP), ACT.Copy, [(m_pe, "tr")], "tr")
                s("exp", sc_e[:, :], sc_e[:, :], ACT.Exp, [(m_dve, "e2")], "bc")
                s("absd", fac[:, :], B(2), ACT.Abs, [(m_pe, "den")], "den")
                s("hsq", sq[:, 0, :], hm[:, :], ACT.Square, [(m_dve, "h")])
                s("ln", fac[:, :], B(3), ACT.Ln, [(m_pe, "ms")], "ms", bias=eps_c[:, 0:1])
                s("rs", fac[:, :], fac[:, :], ACT.Exp, scale=-0.5)
                go(4 * PARTS)
                s("mixhi", mix_hi[:, bass.ds(it, 1), :].rearrange("p o t -> p (o t)"), mixf[:, :], ACT.Copy, [(m_dve, "mixf")])
            with act.Fori(0, H - 1) as it:
                mlstm(it, False)
            mlstm(H - 1, True)

            act.wait_ge(st_stored, 64 * H + 16)
            act.wait_ge(rows_out, 16 * 4)
            act.wait_ge(m_dve.sem, m_dve.at(H - 1, "mixlo"))
            with act.Fori(0, KT // 4) as it:
                for i in range(4):
                    split_hi(act, Unit(U_O, it, i + 1))
                    w, m = Unit(U_O, it, i), 4 * it + i
                    act.wait_ge(unit_done, w.u)
                    act.wait_ge(o_pe.sem, o_pe.before(m, "ms"))
                    act.wait_ge(o_act.sem, o_act.before(m, "copy"))
                    act.activation(acc_s[:, bass.ds(m, 1), :].rearrange("p o t -> p (o t)"), psum[:, w.slot, 0:T],
                                   ACT.Copy).then_inc(*o_act.step("copy"))
                    act.wait_ge(o_act.sem, o_act.at(m, "copy"))
                    act.activation(fsq[:, 0, :], psum[:, w.slot, 0:T], ACT.Square).then_inc(*o_act.step("sq"))
                    act.wait_ge(o_act.sem, o_act.at(m, "sq"))
                    act.sem_inc(evac_done, 1)

            def n(name, out, in_, fn, need=(), **kw):
                for c, x in need:
                    act.wait_ge(c.sem, c.at(0, x))
                act.wait_ge(n_act.sem, n_act.before(0, name))
                act.activation(out, in_, fn, **kw).then_inc(*n_act.step(name))
            split_hi(act, Unit(U_F, 0, 1))
            act.wait_ge(o_pe.sem, o_pe.at(KT - 1, "ms"))
            n("ln", frb[:, :], psum[:, 2, 0:T], ACT.Ln, scale=1.0 / KT, bias=eps_c[:, 0:1])
            n("r", frb[:, :], frb[:, :], ACT.Exp, scale=-0.5)
            for k in range(KT):
                n(f"sq{k}", fs16[:, k, :], x2[:, k, :], ACT.Square, [(n_pool, f"x{k}")])
                n(f"uh{k}", u_hi[:, k, :], x2[:, k, :], ACT.Copy, scale=norms[:, 2 * KT + k:2 * KT + k + 1])
            split_hi(act, Unit(U_F, 0, 2))
            n("ln2", frb[:, :], psum[:, 4, 0:T], ACT.Ln, [(n_pe, "ms2")], scale=1.0 / KT, bias=eps_c[:, 0:1])
            n("r2", frb[:, :], frb[:, :], ACT.Exp, scale=-0.5)

            def gate_up(group, parity, base, it, i0, per=24, first=False):
                for j in range(4):
                    q = group * 4 + j
                    g, u = (Unit(base, it, i0 + 2 * j + x, per) for x in range(2))
                    if not (first and j == 0):
                        split_hi(act, u)
                        split_hi(act, Unit(base, it, i0 + 2 * j + 2, per))
                    act.wait_ge(f_dve.sem, f_dve.at(q, "g"))
                    act.wait_ge(f_act.sem, f_act.before(q, "e"))
                    act.activation(fs[:, :], fe[:, :], ACT.Exp, scale=-1.0).then_inc(*f_act.step("e"))
                    act.wait_ge(f_act.sem, f_act.before(q, "l"))
                    act.activation(fs[:, :], fs[:, :], ACT.Ln, bias=eps_c[:, 1:2]).then_inc(*f_act.step("l"))
                    act.wait_ge(f_act.sem, f_act.before(q, "s"))
                    act.activation(fs[:, :], fs[:, :], ACT.Exp, scale=-1.0).then_inc(*f_act.step("s"))
                    act.wait_ge(f_dve.sem, f_dve.at(q, "h"))
                    act.wait_ge(f_act.sem, f_act.before(q, "hi"))
                    act.activation(h_hi[:, parity, j, :], fh[:, :], ACT.Copy).then_inc(*f_act.step("hi"))

            def down(base, it, i0, per=24, last=False):
                for n_ in range(3 if last else 4):
                    split_hi(act, Unit(base, it, i0 + n_ + 1, per))
            gate_up(0, 0, U_F, 0, 0, first=True)
            with act.Fori(0, FG // 2) as it:
                for half in range(2):
                    gate_up(Affine(it, 2, 1 + half), 1 - half, U_F + 8, it, 12 * half)
                    down(U_F + 8, it, 12 * half + 8)
            down(U_END - 4, 0, 0, last=True)
            for k in range(KT):
                act.wait_ge(added.sem, added.at(FG - 1, f"{k // 4}{'ab'[k % 4 // 2]}"))
                n(f"fq{k}", fs16[:, k, :], acc_s[:, k, :], ACT.Square)
            n("ln3", frb[:, :], psum[:, 2, 0:T], ACT.Ln, [(n_pe, "ffn")], scale=1.0 / KT, bias=eps_c[:, 0:1])
            n("r3", frb[:, :], frb[:, :], ACT.Exp, scale=-0.5)
            for k in range(KT):
                b = k // 4 % 2
                if k % 4 == 0 and k >= 8:
                    act.wait_ge(y_out[b], 64 * (k // 8))
                act.wait_ge(n_pe.sem, n_pe.at(0, f"y{k}"))
                act.activation(y_tok[:, b, 0:2, k % 4, :], psum[:, 3 + k % 4, 0:2 * P].rearrange("p (t d) -> p t d", t=2), ACT.Copy)
                n(f"yc{k}", y_tok[0:T2, b, 2, k % 4, :], psum[0:T2, 3 + k % 4, 2 * P:TP], ACT.Copy)

        @block.tensor
        def _(pe):
            pe.sem_inc(unit_done, 2)
            for c in (a_pe, g_pe, m_pe, o_pe, n_pe, tail):
                pe.sem_inc(c.sem, c.n)

            def wait(it, *need):
                for c, x in need:
                    pe.wait_ge(c.sem, c.at(it, x))

            def mm(out, a, b, start=True, stop=True):
                return pe.matmul(out, a, b, start=start, stop=stop, skip_group_check=True)

            pe.wait_ge(const_in, 16)
            pe.wait_ge(small_in, 16 * 8)
            pe.transpose(psum[:, 0, 0:80], norm_rows, ident[0:80, 0:80])
            pe.transpose(psum[:, 0, 80:176], tap_rows, ident[0:96, 0:96])
            pe.transpose(psum[:, 0, 176:240], n_rows, ident[0:64, 0:64]).then_inc(*a_pe.step("norms"))
            wait(0, (a_dve, "dg2"))
            for t, s0, n in TILE:
                ins = mm(psum[:, 1, s0:s0 + n], ones, v_tok[:, t, 0:n], start=(t == 0), stop=(t == 2))
            ins.then_inc(*a_pe.step("rb"))
            for k in range(KT + 4):
                if k < KT:
                    if k >= 4:
                        wait(0, (a_act, f"xo{k - 4}"))
                    for t, s0, n in TILE:
                        ins = pe.transpose(psum[:, 2 + k % 4, s0:s0 + n], xtok[0:n, t, k * P:k * P + P], ident[0:n, 0:n])
                    ins.then_inc(*a_pe.step(f"x{k}"))
                if k == CONV_AT:
                    pe.wait_ge(rows_in, 16 * 8)
                    wait(0, (a_act, "ss2"))
                    for ct in range(3 * H):
                        ins = pe.transpose(psum[:, 6 + ct // 12, (ct % 12) * 24:(ct % 12) * 24 + 24],
                                           conv_rows[ct // H][:, (ct % H) * P:(ct % H) * P + P], ident[0:24, 0:24])
                    ins.then_inc(*a_pe.step("conv"))
                if k >= 4:
                    if k == 4:
                        pe.wait_ge(lo_done, U_G)
                        wait(0, (a_dve, "rb"), (a_dve, "n_in"))
                    wait(0, (a_dve, f"ul{k - 4}"))
                    one = lambda w, c: [(whi[w][:, k - 4, 0:c], wlo[w][:, k - 4, 0:c], u_hi[:, k - 4, :], u_lo[:, k - 4, :])]
                    gates_ins = products(pe, psum[0:4 * H, 1, 0:T], one(1, 4 * H), k == 4, k == KT + 3)
                    if k == KT + 3:
                        gates_ins.then_inc(unit_done, 1)
                    ins = products(pe, psum[:, 0, 0:T], one(0, P), k == 4, k == KT + 3)
            ins.then_inc(unit_done, 1)
            wait(0, (a_act, "gates"))
            for q in range(4):
                ins = mm(psum[0:H, 2 + q, 0:T], ident[0:4 * H, q * H:q * H + H], gates[:, :])
            ins.then_inc(*a_pe.step("sel"))
            for i in range(1, 3):
                for part in range(PARTS):
                    unit_part(pe, Unit(U_G, 0, i), part, u_hi, u_lo, lo_done)
            wait(0, (a_dve, "bc"), (a_act, "kh"), (a_act, "wl"))
            for t in range(3):
                for q in range(6):
                    c0 = (t * 6 + q) * H
                    ins = mm(psum[:, 2, c0:c0 + H], col_src[:, q, t * P:t * P + P], ident[0:H, 0:H],
                             start=(t == 0 and q == 0), stop=(t == 2 and q == 5))
            ins.then_inc(*a_pe.step("cols"))
            for part in range(PARTS):
                unit_part(pe, Unit(U_G, 0, 3), part, u_hi, u_lo, lo_done)

            def broadcast():
                for row in range(3):
                    ins = mm(B(row), sel[:, :], rows_g[:, row * T:row * T + T])
                return ins

            def interleave(steps, slots, unit):
                todo = [(slots[name], name, fn) for name, fn in steps]
                for slot in range(4 * PARTS + 1):
                    while todo and (todo[0][0] <= slot or slot == 4 * PARTS):
                        todo.pop(0)[2]()
                    if slot < 4 * PARTS and unit is not None:
                        unit_part(pe, unit(slot // PARTS), slot % PARTS, u_hi, u_lo)

            def gdn(it, last):
                def ss():
                    for c, x in ((g_act, "esq"), (g_act, "oln"), (g_dve, "sp")):
                        pe.wait_ge(c.sem, c.prev(it, x))
                    mm(B(3), ones, sq[:, 0, :])
                    mm(B(5), ones, sq[:, 1, :]).then_inc(*g_pe.step("ss"))

                def kk():
                    wait(it, (g_act, "ln"), (g_dve, "qn"))
                    for t, s0, n in TILE:
                        mm(B(3, s0, s0 + n), kn[:, t * P:t * P + P], kb[:, s0:s0 + n], t == 0, t == 2)
                    for t, s0, n in TILE:
                        ins = mm(B(4, s0, s0 + n), kn[:, t * P:t * P + P], qn[:, s0:s0 + n], t == 0, t == 2)
                    ins.then_inc(*g_pe.step("kk"))

                def tr():
                    wait(it, (g_dve, "kn"))
                    for t in range(3):
                        pe.transpose(B(5, t * P, t * P + P), cs[:, 2, t * P:t * P + P], ident)
                    for t in range(3):
                        ins = pe.transpose(B(0, t * P, t * P + P), kn[:, t * P:t * P + P], ident)
                    ins.then_inc(*g_pe.step("tr"))

                def l0():
                    wait(it, (g_dve, "nat"))
                    for t, s0, n in TILE:
                        ins = mm(B(2, s0, s0 + n), nat[:, t * P:t * P + P], ident[:, 0:n], t == 0, t == 2)
                    ins.then_inc(*g_pe.step("l0"))

                def p(lv):
                    def go():
                        wait(it, (g_dve, f"t{lv - 1}"))
                        for t, s0, n in TILE:
                            ins = mm(B(1, s0, s0 + n), nat[:, t * P:t * P + P], tinv[:, t, 0:n], t == 0, t == 2)
                        ins.then_inc(*g_pe.step(f"p{lv}"))
                    return go

                def q(lv):
                    def go():
                        wait(it, (g_act, f"p{lv}"), (g_dve, f"u{lv - 1}"))
                        for t, s0, n in TILE if lv < LEVELS - 1 else ():
                            mm(B(2, s0, s0 + n), uinv[:, t, :], pb[:, s0:s0 + n], t == 0, t == 2)
                        for t, s0, n in TILE:
                            ins = mm(B(3, s0, s0 + n), pb[:, t * P:t * P + P], uinv[:, t, 0:n], t == 0, t == 2)
                        ins.then_inc(*g_pe.step(f"q{lv}"))
                    return go

                def nkd_():
                    wait(it, (g_dve, f"u{LEVELS - 1}"), (g_dve, "qkd"), (g_dve, "kb2"))
                    for t, s0, n in TILE:
                        ins = mm(B(4, s0, s0 + n), k_tok[:, t, :], uinv[:, t, 0:n], t == 0, t == 2)
                    ins.then_inc(*g_pe.step("nkd"))

                def w0():
                    wait(it, (g_act, "vb2"))
                    mm(B(5, 0, P), uinv[:, 0, :], v_tok[:, 0, :]).then_inc(*g_pe.step("w0"))

                def s1():
                    wait(it, (g_act, "w0"), (g_dve, "kh2"))
                    mm(B(0, 0, P), kh_tok[:, 0, :], wv[:, 0, :]).then_inc(*g_pe.step("s1"))

                def w1():
                    wait(it, (g_dve, "s1"), (g_act, "nkd"))
                    mm(B(5, P, 2 * P), uinv[:, 1, :], v_tok[:, 1, :], True, False)
                    mm(B(5, P, 2 * P), nkd[:, P:2 * P], s_chunk[:, 0, :], False, True).then_inc(*g_pe.step("w1"))

                def s2():
                    wait(it, (g_act, "w1"))
                    mm(B(0, P, 2 * P), kh_tok[:, 1, :], wv[:, 1, :]).then_inc(*g_pe.step("s2"))

                def w2():
                    wait(it, (g_dve, "s2"), (g_dve, "nkdm"))
                    pe.wait_ge(st_loaded, 16 * (it + 1))
                    mm(B(5, 2 * P, 3 * P), uinv[:, 2, :], v_tok[:, 2, :], True, False)
                    out = psum[0:T2, 7, 2 * P:3 * P]
                    for b in range(NB):
                        mm(out, nkdm[:, b, :], st_in[:, b, :], False, False)
                    mm(out, nkdm[:, NB, :], s_chunk[:, 1, :], False, True).then_inc(*g_pe.step("w2"))

                def o():
                    wait(it, (g_act, "w2"), (g_dve, "qeg"))
                    for t, s0, n in TILE:
                        mm(B(4, s0, s0 + n), wv[:, t, :], dec[:, s0:s0 + n], t == 0, False)
                    mm(B(4, P, 2 * P), s_chunk[:, 0, :], qeg[:, P:2 * P], False, False)
                    mm(B(4, 2 * P, NP), s_chunk[:, 1, :], qeg[:, 2 * P:NP], False, False)
                    for b in range(NB):
                        c0 = NP + b * DEC
                        ins = mm(B(4, c0, c0 + DEC), st_in[:, b, :], qeg[:, c0:c0 + DEC], False, b == NB - 1)
                    ins.then_inc(*g_pe.step("o"))

                def st():
                    wait(it, (g_pool, "wm"), (g_dve, f"u{LEVELS - 1}"))
                    for bank, g0, gn in ((1, 0, 4), (2, 4, 4), (3, 8, 1)):
                        ins = mm(B(bank, 0, gn * P), kh_tok[0:T2, 2, :], vm[:, g0:g0 + gn, :])
                    ins.then_inc(*g_pe.step("st"))

                def ms():
                    wait(it, (g_act, "osq"))
                    mm(B(5), mean, fac[:, :]).then_inc(*g_pe.step("ms"))

                def bc():
                    if last:
                        g_pe.skip(pe, it, ["bc"])
                    else:
                        wait(it, (g_pool, "sel"), (g_dve, "so1"))
                        broadcast().then_inc(*g_pe.step("bc"))
                return [("ss", ss), ("kk", kk), ("tr", tr), ("l0", l0)] \
                    + [x for lv in range(1, LEVELS) for x in ((f"p{lv}", p(lv)), (f"q{lv}", q(lv)))] \
                    + [("nkd", nkd_), ("w0", w0), ("s1", s1), ("w1", w1), ("s2", s2), ("w2", w2), ("o", o), ("st", st), ("ms", ms), ("bc", bc)]
            wait(0, (a_act, "esq"))
            pe.wait_ge(a_pool.sem, a_pool.at(0, "sel"))
            broadcast().then_inc(*a_pe.step("bc"))
            with pe.Fori(0, H - 1) as it:
                interleave(gdn(it, False), SLOT_G, lambda i: Unit(U_G, it, 4 + i))
            interleave(gdn(H - 1, True), SLOT_G, lambda i: Unit(U_G, H - 1, 4 + i))

            def mlstm(it):
                def tr():
                    wait(it, (m_act, "vp"))
                    pe.wait_ge(pads_ready, H + 1)
                    for t in range(3):
                        pe.transpose(B(3, t * P, t * P + P), kn[:, t * P:t * P + P], ident)
                    for t in range(3):
                        ins = pe.transpose(B(4, t * P, t * P + P), vpad[:, t * P:t * P + P], ident)
                    ins.then_inc(*m_pe.step("tr"))

                def bc():
                    wait(it, (m_pool, "sel"))
                    pe.wait_ge(m_dve.sem, m_dve.before(it, "o1"))
                    mm(B(0, 0, T + NB * DEC), sel[:, :], rows_m[:, 0:T + NB * DEC])
                    mm(B(1), sel[:, :], rows_m[:, T + NB * DEC:]).then_inc(*m_pe.step("bc"))

                def sc():
                    wait(it, (m_act, "k"))
                    for t, a, b, c0 in ((0, 0, NP, 0), (1, P, NP, NP), (2, 2 * P, T, NP + NP - P)):
                        ins = mm(B(2, c0, c0 + b - a), kn[:, t * P:t * P + P], qn[:, a:b], t == 0, t == 2)
                    ins.then_inc(*m_pe.step("sc"))

                def over_keys(bank, lhs):
                    for t, a, b, c0 in ((0, 0, NP, 0), (1, P, NP, NP), (2, 2 * P, T, NP + NP - P)):
                        mm(B(bank, a, b), lhs(t), sc_p[:, c0:c0 + b - a], t == 0, False)

                def num():
                    wait(it, (m_dve, "pm"), (m_act, "v"), (m_dve, "qi"))
                    pe.wait_ge(st_loaded, 16 * (it + H + 1))
                    over_keys(5, lambda t: v_tok[:, t, :])
                    for b in range(NB):
                        c0 = NP + b * DEC
                        ins = mm(B(5, c0, c0 + DEC), st_in[:, b, :], qi[:, b * DEC:b * DEC + DEC], False, b == NB - 1)
                    ins.then_inc(*m_pe.step("num"))

                def den():
                    wait(it, (m_dve, "nq"))
                    over_keys(2, lambda t: ones)
                    mm(B(2, NP, T), ones, nq[:, :], False, True).then_inc(*m_pe.step("den"))

                def st():
                    wait(it, (m_dve, "kw2"), (m_pool, "vm"), (m_dve, "dmax"))
                    mm(B(4, 0, 4 * P), k_tok[0:T2, 2, :], vm[:, 0:4, :])
                    mm(B(0, 0, 4 * P), k_tok[0:T2, 2, :], vm[:, 4:8, :])
                    mm(B(1, 0, P), k_tok[0:T2, 2, :], vm[:, 8, :], True, False)
                    mm(B(1, P, P + NG), k_tok[0:T2, 2, :], C("gmask", T2), False, False)
                    for t in range(2):
                        mm(B(1, 0, P), k_tok[:, t, :], v_tok[:, t, :], False, False)
                        ins = mm(B(1, P + NB, P + NG), k_tok[:, t, :], ones[:, 0:1], False, t == 1)
                    ins.then_inc(*m_pe.step("st"))

                def ms():
                    wait(it, (m_act, "hsq"))
                    mm(B(3), mean, sq[:, 0, :]).then_inc(*m_pe.step("ms"))
                return [("bc", bc), ("tr", tr), ("sc", sc), ("num", num), ("den", den), ("st", st), ("ms", ms)]
            with pe.Fori(0, H - 1) as it:
                interleave(mlstm(it), SLOT_M, lambda i: Unit(U_M, it, 4 + i))
            interleave(mlstm(H - 1), SLOT_M, None)

            pe.wait_ge(m_dve.sem, m_dve.at(H - 1, "mixlo"))
            for n in range(6):
                if n >= 2:
                    wait(0, (tail_v, f"c{n - 2}"))
                for x in range(4):
                    ct = 4 * n + x
                    ins = pe.transpose(psum[0:NG * 3, 6 + n % 2, x * P:x * P + P], conv_out[:, ct // H, ct % H, :], ident)
                ins.then_inc(*tail.step(f"c{n}"))
            wait(0, (tail_v, "c5"))
            pe.wait_ge(m_dve.sem, m_dve.at(H - 1, "np"))
            pe.transpose(psum[0:NG * H, 6, 0:P], n_out[:, :, :].rearrange("p g h -> p (g h)"), ident).then_inc(*tail.step("n"))

            pe.wait_ge(m_dve.sem, m_dve.at(H - 1, "mixlo"))

            def sum_squares(m):
                wait(m, (o_act, "sq"))
                first = isinstance(m, int) and m == 0
                mm(psum[:, 2, 0:T], mean, fsq[:, 0, :], first, isinstance(m, int) and m == KT - 1).then_inc(*o_pe.step("ms"))

            def o_unit(it, i, sums):
                w = Unit(U_O, it, i)
                pe.wait_ge(lo_pool if isinstance(it, int) and it + i == 0 else lo_done, w.u)
                pe.wait_ge(evac_done, w.u - 2)
                products(pe, psum[:, w.slot, 0:T], tiles(w, range(8), mix_hi, mix_lo), True, False)
                if sums:
                    sum_squares(4 * it + i - 1)
                products(pe, psum[:, w.slot, 0:T], tiles(w, range(8, KT), mix_hi, mix_lo), False, True).then_inc(unit_done, 1)
            for i in range(4):
                o_unit(0, i, i > 0)
            with pe.Fori(1, KT // 4) as it:
                for i in range(4):
                    o_unit(it, i, True)
            sum_squares(KT - 1)

            pe.wait_ge(evac_done, U_F - 1)
            pe.wait_ge(lo_done, U_F + 1)
            for k in range(KT):
                wait(0, (n_act, f"uh{k}"), (n_dve, f"ul{k}"))
                for x in range(2):
                    ins = products(pe, psum[:, x, 0:T], tiles(Unit(U_F, 0, x), [k], u_hi, u_lo), k == 0, k == KT - 1)
                    if k == KT - 1:
                        ins.then_inc(unit_done, 1)
                ins = mm(psum[:, 4, 0:T], mean, fs16[:, k, :], k == 0, k == KT - 1)
            ins.then_inc(*n_pe.step("ms2"))

            def gate_up(group, base, it, i0, per=24, first=False):
                for j in range(1 if first else 0, 4):
                    q = group * 4 + j
                    for x in range(2):
                        w = Unit(base, it, i0 + 2 * j + x, per)
                        pe.wait_ge(lo_done, w.u)
                        if not isinstance(q, int) or q >= 2:
                            pe.wait_ge(f_dve.sem, f_dve.at(q + -2, "g" if x == 0 else "u"))
                        products(pe, psum[:, 2 * (j % 2) + x, 0:T], tiles(w, range(KT), u_hi, u_lo), True, True
                                 ).then_inc(unit_done, 1)

            def down(group, parity, base, it, i0, per=24):
                pe.wait_ge(f_dve.sem, f_dve.at(group * 4 + 3, "lo"))
                for n in range(4):
                    w = Unit(base, it, i0 + n, per)
                    pe.wait_ge(lo_done, w.u)
                    for half, done in (("a", half_done), ("b", unit_done)):
                        pe.wait_ge(added.sem, added.before(group, f"{n}{half}") - 1)
                        for m in (0, 1) if half == "a" else (2, 3):
                            ins = products(pe, psum[:, 4 + m, 0:T],
                                           [(whi[w.slot][:, 4 * k + m, :], wlo[w.slot][:, 4 * k + m, :],
                                             h_hi[:, parity, k, :], h_lo[:, parity, k, :]) for k in range(4)], True, True)
                        ins.then_inc(done, 1)
            gate_up(0, U_F, 0, 0, first=True)
            with pe.Fori(0, FG // 2) as it:
                for half in range(2):
                    gate_up(Affine(it, 2, 1 + half), U_F + 8, it, 12 * half)
                    down(Affine(it, 2, half), half, U_F + 8, it, 12 * half + 8)
            down(FG - 1, 0, U_END - 4, 0, 0)
            for k in range(KT):
                wait(0, (n_act, f"fq{k}"))
                ins = mm(psum[:, 2, 0:T], mean, fs16[:, k, :], k == 0, k == KT - 1)
            ins.then_inc(*n_pe.step("ffn"))
            for k in range(KT):
                if k >= 4:
                    wait(0, (n_act, f"yc{k - 4}"))
                wait(0, (n_pool, f"fx{k}"))
                for t, s0, n in TILE:
                    ins = pe.transpose(psum[0:n, 3 + k % 4, t * P:t * P + P], acc_s[:, k, s0:s0 + n], ident)
                ins.then_inc(*n_pe.step(f"y{k}"))

        @block.vector
        def _(dve):
            dve.sem_inc(lo_done, 2)
            for c in (a_dve, g_dve, m_dve, f_dve, added, n_dve, tail_v):
                dve.sem_inc(c.sem, c.n)

            def runner(own, it):
                def s(name, op, *args, need=(), **kw):
                    for c, x in need:
                        dve.wait_ge(c.sem, c.at(it, x))
                    dve.wait_ge(own.sem, own.before(it, name))
                    if op == dve.copy_predicated:
                        dve.sem_inc(join_turn, 1)
                    op(*args, **kw).then_inc(*own.step(name))
                return s
            copy, tt, ts, stt = dve.tensor_copy, dve.tensor_tensor, dve.tensor_scalar, dve.scalar_tensor_tensor

            a = runner(a_dve, 0)
            dve.memset(ssum[:, :], 1.0)
            for n, v in enumerate((EPS, 1.0, float(np.log(QS)))):
                dve.memset(eps_c[:, n:n + 1], v)
            a("ones", dve.memset, m8[:, :], 0.0)
            a("norms", copy, norms[:, :], psum[:, 0, 0:80], need=[(a_pe, "norms")])
            a("convw", copy, convw[:, :], psum[:, 0, 80:176])
            a("n_in", copy, n_in[:, :], psum[:, 0, 176:240])
            for t in range(3):
                a(f"dg{t}", ts, v_tok[:, t, :], ident, ssum[:, t:t + 1], None, ALU.mult, need=[(a_act, "r")])
            a("rb", copy, fac[:, :], psum[:, 1, 0:T], need=[(a_pe, "rb")])
            for k in range(KT + 1):
                if k == SPLIT_AT:
                    dve.wait_ge(hi_done, 3)
                    dve.tensor_tensor(wlo[1][:, :, 0:4 * H], raw[:, 1, :, 0:4 * H], whi[1][:, :, 0:4 * H].bitcast(F32),
                                      ALU.subtract).then_inc(lo_done, 1)
                    split_lo(dve, Unit(U_G, 0, 0))
                if k < KT:
                    if k >= 2:
                        dve.wait_ge(a_act.sem, a_act.at(0, f"uh{k - 2}"))
                    a(f"ut{k}", stt, sq[:, k % 2, :], x_out[:, k % 3, :], norms[:, k:k + 1], fac[:, :], ALU.mult, ALU.mult,
                      need=[(a_act, f"xo{k}")])
                if k >= 1:
                    a(f"ul{k - 1}", tt, u_lo[:, k - 1, :], sq[:, (k - 1) % 2, :], u_hi[:, k - 1, :].bitcast(F32), ALU.subtract,
                      need=[(a_act, f"uh{k - 1}")])
            for n in range(2):
                flat = conv_in[:, :, :, :].rearrange("p c h r -> p (c h r)")
                a(f"ci{n}", copy, flat[:, 288 * n:288 * n + 288], psum[:, 6 + n, 0:288], need=[(a_pe, "conv")])
            split_lo(dve, Unit(U_G, 0, 1))
            dve.wait_ge(rows_in, 16 * 8)
            bias = lambda n: bias8[:, n:n + 1]
            a("li", ts, li[:, :], psum[0:H, 2, 0:T], bias(0), None, ALU.add, need=[(a_pe, "sel")])
            a("yf0", ts, yf[:, 0, :], psum[0:H, 3, 0:T], bias(1), None, ALU.add)
            a("yf1", ts, yf[:, 1, :], psum[0:H, 4, 0:T], bias(2), None, ALU.add)
            split_lo(dve, Unit(U_G, 0, 2))
            G_, BT, EG = (rows_g[:, n * T:n * T + T] for n in range(3))
            R_, IN = rows_m[:, 0:T], rows_m[:, T:T + NB * DEC]
            a("b1", ts, BT, BT, 1.0, None, ALU.add, need=[(a_act, "bexp")])
            a("b2", dve.reciprocal, BT, BT)
            a("lf", stt, yf[:, 0, :], yf[:, 0, :], 0.0, la[:, 0, :], ALU.min, ALU.subtract, need=[(a_act, "aln")])
            a("sp", stt, yf[:, 1, :], yf[:, 1, :], 0.0, la[:, 1, :], ALU.max, ALU.add)
            a("lg", ts, yf[:, 1, :], yf[:, 1, :], decay[:, 0:1], -1.0, ALU.mult, ALU.mult)
            dve.wait_ge(st_stored, 16)
            a("bsc", dve.tensor_tensor_scan, b_row[:, :], scan_m[:, 0, :], yf[:, 0, :], 0.0, ALU.mult, ALU.add)
            a("gsc", dve.tensor_tensor_scan, G_, scan_m[:, 1, :], yf[:, 1, :], 0.0, ALU.mult, ALU.add)
            dve.wait_ge(a_pool.sem, a_pool.at(0, "z2"))
            a("c", tt, col_src[:, 0, 0:T], li[:, :], b_row[:, :], ALU.subtract)
            lf0, li0 = group_cols(yf[:, 0, :])[:, :, 0], group_cols(li)[:, :, 0]
            a("mx0", tt, li[:, 0:1], li[:, 0:1], yf[:, 0, 0:1], ALU.max)
            a("t8", tt, m8[:, :], lf0, mp[:, :], ALU.add)
            a("mx1", tt, li0, li0, m8[:, :], ALU.max)
            a("ng0", dve.memset, yf[:, 0, 0:1], NEG)
            a("ng1", dve.memset, lf0, NEG)
            a("msc", dve.tensor_tensor_scan, m_row[:, :], yf[:, 0, :], li[:, :], 0.0, ALU.add, ALU.max)
            a("r", tt, R_, b_row[:, :], m_row[:, :], ALU.subtract)
            spread_g = lambda x: x.unsqueeze(2).to_broadcast([H, NB, DEC])
            a("it", tt, group_cols(IN, 0), group_cols(R_), spread_g(mp[:, :]), ALU.add)
            end = lambda x: group_cols(x)[:, :, DEC - 1]
            a("wl0", ts, col_src[:, 1, 0:NP], col_src[:, 0, 0:NP], R_[:, NP - 1:NP], None, ALU.add)
            a("wl1", tt, group_cols(col_src[:, 1, :]), group_cols(col_src[:, 0, :]), spread_g(end(R_)), ALU.add)
            a("ngg", ts, col_src[:, 2, 0:T], G_, -1.0, None, ALU.mult)
            for n, (x, z) in enumerate(((0, P), (P, 2 * P), (2 * P, NP))):
                a(f"kh{n}", ts, col_src[:, 5, x:z], G_[:, x:z], -1.0, G_[:, z - 1:z], ALU.mult, ALU.add)
            a("kh3", tt, group_cols(col_src[:, 5, :]), spread_g(end(G_)), group_cols(G_), ALU.subtract)
            a("nb", stt, col_src[:, 3, 0:T], BT, -1.0, EG, ALU.mult, ALU.mult, need=[(a_act, "eg")])
            a("bc", copy, col_src[:, 4, 0:T], BT)
            split_lo(dve, Unit(U_G, 0, 3))
            a("cols", copy, cols[:, :, :, :].rearrange("p t q h -> p (t q h)"), psum[:, 2, 0:144], need=[(a_pe, "cols")])

            flat3 = lambda x: x[:, :, :].rearrange("p t n -> p (t n)")

            def convolve(s, c, head, taps):
                for i in taps:
                    w = convw[:, bass.ds(head + (i * 3 * H + c * H), 1)]
                    if i == 0:
                        s(f"c{c}w0", ts, y[:, c, :], stage[:, c, 0:YW], w, None, ALU.mult)
                    else:
                        s(f"c{c}w{i}", stt, y[:, c, :], stage[:, c, i:i + YW], w, y[:, c, :], ALU.mult, ALU.add)

            def silu(s, ac):
                s("cs_p", tt, cs[:, :, 0:NP], cs[:, :, 0:NP], y[:, :, 0:NP], ALU.mult, need=[(ac, "e2s")])
                for c in range(3):
                    args = group_cols(cs[:, c, :]), group_cols(cs[:, c, :]), conv_groups(y[:, c, :]), ALU.mult
                    if c < 2:
                        dve.tensor_tensor(*args)
                    else:
                        s("cs_d", tt, *args)
            dve.wait_ge(pads_ready, 1)
            for c in range(3):
                dve.wait_ge(evac_done, Unit(U_G, 0, c).u)
                convolve(a, c, 0, range(TAPS))
            dve.wait_ge(a_pool.sem, a_pool.at(0, "ui"))
            silu(a, a_act)
            dve.wait_ge(a_pe.sem, a_pe.at(0, "bc"))

            def gdn(it, last):
                nxt = [Unit(U_G, it, 4 + i) for i in range(3)]
                s = runner(g_dve, it)

                def next_conv(c, taps):
                    if last:
                        g_dve.skip(dve, it, [f"c{c}w{i}" for i in taps])
                        return
                    if taps[0] == 0:
                        dve.wait_ge(evac_done, nxt[c].u)
                        dve.wait_ge(pads_ready, it + 2)
                    convolve(s, c, it + 1, taps)
                dve.wait_ge(g_pe.sem, g_pe.prev(it, "bc"))
                for t, s0, n in TILE:
                    s(f"e{t}", stt, dec[:, s0:s0 + n], B(0, s0, s0 + n), cols[:, t, 2, bass.ds(it, 1)],
                      C("cap_g")[:, s0:s0 + n], ALU.add, ALU.min)
                s("kn", tt, kn[:, 0:T], cs[:, 1, 0:T], sq[:, 1, :], ALU.mult, need=[(g_act, "rs")])
                s("kb", tt, kb[:, :], kn[:, 0:T], B(1), ALU.mult)
                s("qn", stt, qn[:, :], cs[:, 0, 0:T], QS, sq[:, 0, :], ALU.mult, ALU.mult)
                s("qeg", tt, qeg[:, :], qn[:, :], B(2), ALU.mult)
                s("d1", copy, dcs[:, 0:1], B(2, 2 * P - 1, 2 * P))
                s("d2", copy, dcs[:, 1:2], B(2, NP - 1, NP))
                s("d3", copy, dcs[:, 2:2 + NB], group_cols(B(2))[:, :, DEC - 1])
                s("nat", tt, nat[:, 0:T], decn[:, :], B(3), ALU.mult, need=[(g_pe, "kk"), (g_pool, "decn")])

                def join(lv):
                    mask = lambda n: joins[:, n, :]
                    t_src, u_src, by = (B(2), nat[:, 0:T], "l0") if lv == 0 else (B(2), B(3), f"q{lv}")
                    dve.wait_ge(g_pe.sem, g_pe.at(it, by))
                    if lv < LEVELS - 1:
                        s(f"t{lv}", dve.copy_predicated, flat3(tinv)[:, 0:T], mask(lv), t_src)
                    s(f"u{lv}", dve.copy_predicated, flat3(uinv)[:, 0:T], mask(LEVELS + lv), u_src)
                dve.wait_ge(g_pool.sem, g_pool.prev(it, "ui"))
                join(0)
                s("qkd", tt, dec[:, :], dec[:, :], B(4), ALU.mult)
                for t in range(3):
                    s(f"kb{t}", ts, k_tok[:, t, :], B(0, t * P, t * P + P), cols[:, t, 3, bass.ds(it, 1)], None, ALU.mult,
                      need=[(g_pe, "tr")])
                join(1)
                for t in range(3):
                    s(f"kh{t}", ts, kh_tok[:, t, :], B(0, t * P, t * P + P), cols[:, t, 5, bass.ds(it, 1)], None, ALU.mult)
                s("gate", tt, gate[:, :], gate[:, :], stage_z[:, :], ALU.mult, need=[(g_act, "z2")])
                join(2)
                for lv in range(3, LEVELS):
                    next_conv((lv - 3) // 2, (0, 1) if lv % 2 else (2, 3))
                    join(lv)
                s("nkdm", tt, nkdm[:, :, :], nkd[:, 2 * P:T].unsqueeze(1).to_broadcast([P, NG, T2]),
                  C("gmask_rows").rearrange("p (g t) -> p g t", g=NG), ALU.mult, need=[(g_act, "nkd")])
                s("s1", copy, s_chunk[:, 0, :], B(0, 0, P), need=[(g_pe, "s1")])
                next_conv(2, (0, 1))
                s("s2", stt, s_chunk[:, 1, :], s_chunk[:, 0, :], dcs[:, 0:1], B(0, P, 2 * P), ALU.mult, ALU.add,
                  need=[(g_pe, "s2")])
                next_conv(2, (2, 3))
                if last:
                    g_dve.skip(dve, it, ["cs_p", "cs_d"])
                else:
                    silu(s, g_act)
                for n in range(2):
                    s(f"so{n}", tt, st_out[:, 4 * n:4 * n + 4, :], st_out[:, 4 * n:4 * n + 4, :],
                      B(1 + n, 0, 512).rearrange("p (g e) -> p g e", g=4), ALU.add, need=[(g_pe, "st"), (g_pool, "sdec")])
                dve.wait_ge(st_stored, 32 * it + 16)
                s("sp", stt, st_out[:, NB, :], s_chunk[:, 1, :], dcs[:, 1:2], B(3, 0, P), ALU.mult, ALU.add)
                s("omul", stt, mixf[:, :], B(4), norms[:, bass.ds(72 + it, 1)], fac[:, :], ALU.mult, ALU.mult,
                  need=[(g_act, "ors")])
                s("omix", tt, mixf[:, :], mixf[:, :], gate[:, :], ALU.mult)
                s("mixlo", tt, mix_lo[:, bass.ds(it + H, 1), :].rearrange("p o t -> p (o t)"), mixf[:, :],
                  mix_hi[:, bass.ds(it + H, 1), :].rearrange("p o t -> p (o t)").bitcast(F32), ALU.subtract, need=[(g_act, "mixhi")])
            with dve.Fori(0, H - 1) as it:
                gdn(it, False)
            gdn(H - 1, True)

            def mlstm(it):
                s = runner(m_dve, it)
                s("o1", ts, gate[:, :], gate[:, :], 1.0, None, ALU.add, need=[(m_act, "oe")])
                s("gate", dve.reciprocal, gate[:, :], gate[:, :])
                col = lambda t, q: cols[:, t, q, bass.ds(it, 1)]
                for t, x, z, c0 in ((0, 0, NP, 0), (1, P, NP, NP), (2, 2 * P, T, NP + NP - P)):
                    s(f"e{t}", stt, sc_e[:, c0:c0 + z - x], B(0, x, z), col(t, 0), C("cap_m")[:, c0:c0 + z - x],
                      ALU.add, ALU.min, need=[(m_pe, "bc")])
                for t in range(3):
                    s(f"kw{t}", ts, k_tok[:, t, :], B(3, t * P, t * P + P), col(t, 1), None, ALU.mult, need=[(m_pe, "tr")])
                s("pm", tt, sc_p[:, :], sc_e[:, :], B(2, 0, 464), ALU.mult, need=[(m_act, "exp"), (m_pe, "sc")])
                s("qi", tt, qi[:, :], qn[:, NP:T], B(0, T, T + NB * DEC), ALU.mult)
                s("nq", tt, group_cols(nq, 0), group_cols(qi, 0),
                  n_in[:, :].rearrange("p (b h) -> p b h", h=H)[:, :, bass.ds(it, 1)].to_broadcast([P, NB, DEC]), ALU.mult)
                s("dcp", copy, dcs[:, 0:NB], group_cols(B(0, T, T + NB * DEC), 0)[:, :, DEC - 1])
                s("dmax", tt, fac[:, :], fac[:, :], B(1), ALU.max, need=[(m_act, "absd")])
                s("drec", dve.reciprocal, fac[:, :], fac[:, :])
                s("h", tt, hm[:, :], fac[:, :], B(5), ALU.mult)
                s("nm", tt, nm[:, :], n_in[:, :].rearrange("p (b h) -> p b h", h=H)[:, :, bass.ds(it, 1)].rearrange("p b o -> p (b o)"),
                  dcs[:, 0:NB], ALU.mult)
                n_at = lambda g0, g1: n_out[:, g0:g1, bass.ds(it, 1)].rearrange("p g o -> p (g o)")
                s("na", tt, n_at(0, NB), nm[:, :], B(1, P, P + NB), ALU.add, need=[(m_pe, "st")])
                s("np", copy, n_at(NB, NG), B(1, P + NB, P + NG))
                for n in range(2):
                    s(f"co{n}", tt, st_out[:, 4 * n:4 * n + 4, :], st_out[:, 4 * n:4 * n + 4, :],
                      B(4 * (1 - n), 0, 512).rearrange("p (g e) -> p g e", g=4), ALU.add, need=[(m_pool, "cdec")])
                dve.wait_ge(st_stored, 32 * it + 32 * H + 16)
                s("cp", copy, st_out[:, NB, :], B(1, 0, P))
                s("fg", tt, fac[:, :], fac[:, :], gate[:, :], ALU.mult, need=[(m_act, "rs")])
                s("mixf", stt, mixf[:, :], hm[:, :], norms[:, bass.ds(64 + it, 1)], fac[:, :], ALU.mult, ALU.mult)
                s("mixlo", tt, mix_lo[:, bass.ds(it, 1), :].rearrange("p o t -> p (o t)"), mixf[:, :],
                  mix_hi[:, bass.ds(it, 1), :].rearrange("p o t -> p (o t)").bitcast(F32), ALU.subtract, need=[(m_act, "mixhi")])
            dve.wait_ge(pads_ready, H + 1)
            with dve.Fori(0, H) as it:
                mlstm(it)

            s = runner(tail_v, 0)
            for n in range(6):
                s(f"c{n}", copy, conv_back[:, 512 * n:512 * n + 512], psum[0:NG * 3, 6 + n % 2, 0:512], need=[(tail, f"c{n}")])
            s("n", copy, k_tok[0:NG * H, 0, :], psum[0:NG * H, 6, 0:P], need=[(tail, "n")])

            dve.wait_ge(lo_pool, U_O)
            dve.sem_inc(lo_done, U_O - U_G - 3)
            with dve.Fori(0, KT // 4) as it:
                for i in range(4):
                    split_lo(dve, Unit(U_O, it, i + 1))

            split_lo(dve, Unit(U_F, 0, 1))
            s = runner(n_dve, 0)
            weight = lambda n, k: norms[:, n * KT + k:n * KT + k + 1]
            for k in range(KT + 2):
                if k < KT:
                    if k >= 2:
                        dve.wait_ge(n_pool.sem, n_pool.at(0, f"x{k - 2}"))
                    s(f"t{k}", stt, fsq[:, k % 2, :], acc_s[:, k, :], weight(1, k), frb[:, :], ALU.mult, ALU.mult,
                      need=[(n_act, "r")])
                if k >= 2:
                    s(f"ul{k - 2}", stt, u_lo[:, k - 2, :], x2[:, k - 2, :], weight(2, k - 2), u_hi[:, k - 2, :].bitcast(F32),
                      ALU.mult, ALU.subtract, need=[(n_act, f"uh{k - 2}")])

            def gate_up(group, parity, base, it, i0, per=24, first=False):
                for j in range(4):
                    q = group * 4 + j
                    bank = 2 * (j % 2)
                    if first and j == 0:
                        split_lo(dve, Unit(U_F, 0, 2))
                        dve.wait_ge(n_act.sem, n_act.at(0, "r2"))
                    else:
                        split_lo(dve, Unit(base, it, i0 + 2 * j + 1, per))
                    s = runner(f_dve, q)
                    dve.wait_ge(unit_done, Unit(base, it, i0 + 2 * j, per).u)
                    s("g", tt, fe[:, :], psum[:, bank, 0:T], frb[:, :], ALU.mult)
                    if not (first and j == 0):
                        split_lo(dve, Unit(base, it, i0 + 2 * j + 2, per))
                    s("a", tt, fe[:, :], fe[:, :], fs[:, :], ALU.mult, need=[(f_act, "s")])
                    dve.wait_ge(unit_done, Unit(base, it, i0 + 2 * j + 1, per).u)
                    s("u", tt, fh[:, :], psum[:, bank + 1, 0:T], frb[:, :], ALU.mult)
                    s("h", tt, fh[:, :], fh[:, :], fe[:, :], ALU.mult)
                    s("lo", tt, h_lo[:, parity, j, :], fh[:, :], h_hi[:, parity, j, :].bitcast(F32), ALU.subtract,
                      need=[(f_act, "hi")])

            def down(group, base, it, i0, per=24, last=False):
                for n in range(4):
                    if not (last and n == 3):
                        split_lo(dve, Unit(base, it, i0 + n + 1, per))
                    for m, half in ((0, "a"), (2, "b")):
                        if half == "a":
                            dve.wait_ge(half_done, value(group * 4 + (n + 1)))
                        else:
                            dve.wait_ge(unit_done, Unit(base, it, i0 + n, per).u)
                        dve.wait_ge(acc_zero, 1)
                        dve.wait_ge(added.sem, added.before(group, f"{n}{half}"))
                        dve.tensor_tensor(acc_s[:, 4 * n + m:4 * n + m + 2, :], acc_s[:, 4 * n + m:4 * n + m + 2, :],
                                          psum[:, 4 + m:6 + m, 0:T], ALU.add).then_inc(*added.step(f"{n}{half}"))
            gate_up(0, 0, U_F, 0, 0, first=True)
            with dve.Fori(0, FG // 2) as it:
                for half in range(2):
                    gate_up(Affine(it, 2, 1 + half), 1 - half, U_F + 8, it, 12 * half)
                    down(Affine(it, 2, half), U_F + 8, it, 12 * half + 8)
            down(FG - 1, U_END - 4, 0, 0, last=True)

            s = runner(n_dve, 0)
            for k in range(KT):
                if k >= 2:
                    dve.wait_ge(n_pool.sem, n_pool.at(0, f"fx{k - 2}"))
                s(f"ft{k}", stt, fsq[:, k % 2, :], acc_s[:, k, :], weight(3, k), frb[:, :], ALU.mult, ALU.mult,
                  need=[(n_act, "r3")])


INPUTS = ("x_prompt", "x_sample", "state_mlstm_C", "state_mlstm_n", "state_mlstm_m", "state_gdn_S", "state_gdn_conv",
          "meta_tokens", "norm_pre_mix", "norm_post_mix", "norm_pre_ffn", "norm_post_ffn", "w_in", "mlstm_b_i", "mlstm_b_f",
          "mlstm_norm", "gdn_conv_w", "gdn_A_log", "gdn_dt_bias", "gdn_norm", "w_out", "w_gate_up", "w_down")
OUTPUTS = (("y_p", (1, SEQ, D)), ("y_s", (NB, DEC, D)),
           ("p_C", (1, 1, H, P, P)), ("p_n", (1, 1, H, P)), ("p_m", (1, 1, H)), ("p_S", (1, 1, H, P, P)), ("p_conv", (1, 1, 3, 3 * W1)),
           ("s_C", (1, NB, H, P, P)), ("s_n", (1, NB, H, P)), ("s_m", (1, NB, H)), ("s_S", (1, NB, H, P, P)),
           ("s_conv", (1, NB, 3, 3 * W1)))


def kernel(**inputs):
    import concourse.bacc as bacc
    from concourse.bass_utils import run_bass_kernel_spmd

    nc = bacc.Bacc("TRN2", target_bir_lowering=False, num_devices=1)
    table, _, joins, scan_mask = constant_tables()
    arrays = {name: np.ascontiguousarray(inputs[name]) for name in INPUTS}
    arrays |= {"table": table, "joins": joins, "scan_mask": scan_mask}
    A = {name: nc.dram_tensor(f"in_{name}", a.shape, mybir.dt.from_np(a.dtype), kind="ExternalInput").ap()
         for name, a in arrays.items()}
    O = {name: nc.dram_tensor(f"out_{name}", shape, F32, kind="ExternalOutput").ap() for name, shape in OUTPUTS}
    build_layer(nc, A, O)
    r = run_bass_kernel_spmd(nc, [{f"in_{k}": v for k, v in arrays.items()}], core_ids=[0])
    return tuple(r.results[0][f"out_{name}"] for name, _ in OUTPUTS)
```
